# Optimizing a Trainium2 kernel written in Bass

```python
import math
import jax, jax.numpy as jnp
from jax import lax
import numpy as np

D_MODEL = 1024
BATCH = 1
SEQ = 256
DEPTH = 1

RMS_EPS = 1e-6
N_MIX_GROUPS = 4
GROUP_W = D_MODEL // N_MIX_GROUPS
D_MIX = N_MIX_GROUPS * GROUP_W

HGRN_HEADS = 4
HGRN_DK = GROUP_W // HGRN_HEADS
HGRN_DV = GROUP_W // HGRN_HEADS
HGRN_CHUNK = 64

S5_CH = 16
S5_GROUPS = GROUP_W // S5_CH
S5_STATE = 64
S5_DT_MIN = 1e-3
S5_DT_MAX = 1e-1

RWKV_HS = 64
RWKV_HEADS = GROUP_W // RWKV_HS
RWKV_W_LORA = 64
RWKV_A_LORA = 64
RWKV_V_LORA = 32
RWKV_G_LORA = 128
RWKV_GN_EPS = 64e-5
RWKV_SIZES = (GROUP_W, GROUP_W, GROUP_W, RWKV_W_LORA, RWKV_A_LORA, RWKV_G_LORA)
RWKV_COLS = 3 * GROUP_W + RWKV_W_LORA + RWKV_A_LORA + RWKV_G_LORA

LRU_HEADS = 4
LRU_HD = GROUP_W // LRU_HEADS
LRU_CONV = 4
LRU_C = 8.0

MOE_GROUPS = 4
MOE_PER_GROUP = 8
N_EXPERTS = MOE_GROUPS * MOE_PER_GROUP
MOE_TOPK = 2
D_EXPERT = 512

COL_SIZES = (GROUP_W, GROUP_W, GROUP_W, GROUP_W, GROUP_W, RWKV_COLS, GROUP_W, GROUP_W)
D_IN = 7 * GROUP_W + RWKV_COLS

kernel_name = "hybrid_parallel_heads_hier_moe"

def _splits(sizes):
    return np.cumsum(np.array(sizes))[:-1].tolist()

def rms_norm(x, w, eps=RMS_EPS):
    xf = x.astype(jnp.float32)
    y = xf * lax.rsqrt(jnp.mean(xf * xf, axis=-1, keepdims=True) + eps)
    return (y * w.astype(jnp.float32)).astype(x.dtype)

def _shift(p):
    return jnp.pad(p, ((0, 0), (1, 0), (0, 0)))[:, :-1]

def hgrn2_mixer(q_raw, f_raw, i_raw, g_raw, lb, norm_w):
    f32 = jnp.float32
    B, T, _ = q_raw.shape
    n_chunks = T // HGRN_CHUNK
    q = jax.nn.silu(q_raw.astype(f32))
    fx = f_raw.astype(f32)
    log_f = jnp.logaddexp(jnp.log(lb), jnp.log1p(-lb) + jax.nn.log_sigmoid(fx))
    k = (1.0 - lb) * jax.nn.sigmoid(-fx)
    v = jax.nn.silu(i_raw.astype(f32))

    def to_chunks(t, d):
        return t.reshape(B, n_chunks, HGRN_CHUNK, HGRN_HEADS, d).transpose(1, 0, 3, 2, 4)

    tri = jnp.tril(jnp.ones((HGRN_CHUNK, HGRN_CHUNK), dtype=bool))

    def chunk_step(S, inp):
        qc, lfc, kc, vc = inp
        b = jnp.cumsum(lfc, axis=2)
        rel = b[:, :, :, None, :] - b[:, :, None, :, :]
        decay = jnp.exp(jnp.where(tri[:, :, None], rel, -jnp.inf))
        scores = jnp.einsum('bhtk,bhsk,bhtsk->bhts', qc, kc, decay)
        o = (jnp.einsum('bhts,bhsv->bhtv', scores, vc)
             + jnp.einsum('bhtk,bhkv->bhtv', qc * jnp.exp(b), S))
        b_end = b[:, :, -1:, :]
        S = (jnp.exp(b_end[:, :, 0, :])[..., None] * S
             + jnp.einsum('bhsk,bhsv->bhkv', kc * jnp.exp(b_end - b), vc))
        return S, o

    S0 = jnp.zeros((B, HGRN_HEADS, HGRN_DK, HGRN_DV), f32)
    _, o = lax.scan(chunk_step, S0, (to_chunks(q, HGRN_DK), to_chunks(log_f, HGRN_DK),
                                     to_chunks(k, HGRN_DK), to_chunks(v, HGRN_DV)))
    o = o.transpose(1, 0, 3, 2, 4).reshape(B, T, HGRN_HEADS, HGRN_DV)
    o = o * lax.rsqrt(jnp.mean(o * o, axis=-1, keepdims=True) + RMS_EPS)
    o = o * norm_w.astype(f32).reshape(HGRN_HEADS, HGRN_DV)
    o = o.reshape(B, T, GROUP_W) * jax.nn.silu(g_raw.astype(f32))
    return o.astype(q_raw.dtype)

def s5_mixer(u, lam_re, lam_im, log_dt, b_re, b_im, c_re, c_im, d_skip, w_glu):
    f32 = jnp.float32
    B, T, _ = u.shape
    uf = u.astype(f32)
    ug = uf.reshape(B, T, S5_GROUPS, S5_CH)
    lr, li = lam_re.astype(f32), lam_im.astype(f32)
    dt = jnp.exp(log_dt.astype(f32))[:, None]
    mag = jnp.exp(lr * dt)
    a_re, a_im = mag * jnp.cos(li * dt), mag * jnp.sin(li * dt)
    den = lr * lr + li * li
    kap_re = ((a_re - 1.0) * lr + a_im * li) / den
    kap_im = (a_im * lr - (a_re - 1.0) * li) / den
    br, bi = b_re.astype(f32), b_im.astype(f32)
    bb_re = kap_re[..., None] * br - kap_im[..., None] * bi
    bb_im = kap_re[..., None] * bi + kap_im[..., None] * br
    bu_re = jnp.einsum('btgc,gpc->tbgp', ug, bb_re)
    bu_im = jnp.einsum('btgc,gpc->tbgp', ug, bb_im)
    a_re_t = jnp.broadcast_to(a_re, (T, 1, S5_GROUPS, S5_STATE))
    a_im_t = jnp.broadcast_to(a_im, (T, 1, S5_GROUPS, S5_STATE))

    def combine(e1, e2):
        a1r, a1i, b1r, b1i = e1
        a2r, a2i, b2r, b2i = e2
        return (a2r * a1r - a2i * a1i, a2r * a1i + a2i * a1r,
                a2r * b1r - a2i * b1i + b2r, a2r * b1i + a2i * b1r + b2i)

    _, _, x_re, x_im = lax.associative_scan(combine, (a_re_t, a_im_t, bu_re, bu_im), axis=0)
    y = (jnp.einsum('tbgp,gcp->btgc', x_re, c_re.astype(f32))
         - jnp.einsum('tbgp,gcp->btgc', x_im, c_im.astype(f32))).reshape(B, T, GROUP_W)
    y = jax.nn.gelu(y + d_skip * uf)
    za, zb = jnp.split(y @ w_glu.astype(f32), 2, axis=-1)
    return (za * jax.nn.sigmoid(zb)).astype(u.dtype)

def rwkv7_mixer(p, mu, w0, w2, a0, a2, g2, k_k, k_a, r_k, ln_w, ln_b, v_first, v_mix):
    f32 = jnp.float32
    B, T, _ = p.shape
    pf = p.astype(f32)
    pf = pf + mu * (_shift(pf) - pf)
    r, k, v, wd, ad, gd = jnp.split(pf, _splits(RWKV_SIZES), axis=-1)
    w = -jax.nn.softplus(-(w0 + jnp.tanh(wd) @ w2)) - 0.5
    decay = jnp.exp(-jnp.exp(w))
    a = jax.nn.sigmoid(a0 + ad @ a2)
    g = jax.nn.sigmoid(gd) @ g2

    def heads(t):
        return t.reshape(B, T, RWKV_HEADS, RWKV_HS)

    kk = heads(k * k_k)
    kk = kk / jnp.maximum(jnp.sqrt(jnp.sum(kk * kk, axis=-1, keepdims=True)), 1e-12)
    k = k * (1.0 + (a - 1.0) * k_a)
    if v_mix is None:
        v_first = v
    else:
        v0, v1, v2 = v_mix
        v = v + (v_first - v) * jax.nn.sigmoid(v0 + (v @ v1) @ v2)
    rh, kh, vh = heads(r), heads(k), heads(v)
    bh = kk * heads(a)

    def tm(t):
        return t.transpose(1, 0, 2, 3)

    def step(S, inp):
        r_t, w_t, k_t, v_t, kk_t, b_t = inp
        sa = jnp.einsum('bhvk,bhk->bhv', S, -kk_t)
        S = (S * w_t[:, :, None, :] + sa[..., None] * b_t[:, :, None, :]
             + v_t[..., None] * k_t[:, :, None, :])
        return S, jnp.einsum('bhvk,bhk->bhv', S, r_t)

    S0 = jnp.zeros((B, RWKV_HEADS, RWKV_HS, RWKV_HS), f32)
    _, y = lax.scan(step, S0, (tm(rh), tm(heads(decay)), tm(kh), tm(vh), tm(kk), tm(bh)))
    y = y.transpose(1, 0, 2, 3)
    mean = jnp.mean(y, axis=-1, keepdims=True)
    var = jnp.mean((y - mean) ** 2, axis=-1, keepdims=True)
    y = ((y - mean) * lax.rsqrt(var + RWKV_GN_EPS) * ln_w.reshape(RWKV_HEADS, RWKV_HS)
         + ln_b.reshape(RWKV_HEADS, RWKV_HS))
    y = y + jnp.sum(rh * kh * r_k.reshape(RWKV_HEADS, RWKV_HS), axis=-1, keepdims=True) * vh
    out = y.reshape(B, T, GROUP_W) * g
    return out.astype(p.dtype), v_first

def rglru_mixer(xg, xr, conv_w, conv_b, wa, ba, wx, bx, lam):
    f32 = jnp.float32
    B, T, _ = xr.shape
    xc = lax.conv_general_dilated(xr.astype(f32), conv_w.astype(f32)[:, None, :], window_strides=(1,),
                                  padding=[(LRU_CONV - 1, 0)], dimension_numbers=('NWC', 'WIO', 'NWC'),
                                  feature_group_count=GROUP_W) + conv_b
    xh = xc.reshape(B, T, LRU_HEADS, LRU_HD)
    r = jax.nn.sigmoid(jnp.einsum('bthi,hij->bthj', xh, wa).reshape(B, T, GROUP_W) + ba)
    gi = jax.nn.sigmoid(jnp.einsum('bthi,hij->bthj', xh, wx).reshape(B, T, GROUP_W) + bx)
    log_a = -LRU_C * r * jax.nn.softplus(-lam)
    u = jnp.sqrt(-jnp.expm1(2.0 * log_a)) * (gi * xc)

    def combine(e1, e2):
        a1, b1 = e1
        a2, b2 = e2
        return (a1 * a2, a2 * b1 + b2)

    _, h = lax.associative_scan(combine, (jnp.exp(log_a), u), axis=1)
    return (jax.nn.gelu(xg.astype(f32)) * h).astype(xg.dtype)

def hier_moe(h, coarse_w, coarse_b, fine_w, fine_b, w_gate, w_up, w_down):
    B, T, D = h.shape
    xt = h.reshape(B * T, D)
    coarse = (xt @ coarse_w + coarse_b).astype(jnp.float32)
    p_coarse = jax.nn.softmax(coarse, axis=-1)
    gsel = jnp.argmax(coarse, axis=-1)
    g_onehot = jax.nn.one_hot(gsel, MOE_GROUPS, dtype=jnp.float32)
    p_g = jnp.sum(p_coarse * g_onehot, axis=-1, keepdims=True)
    fine = (jnp.einsum('nd,gde->nge', xt, fine_w) + fine_b).astype(jnp.float32)
    fine_sel = jnp.einsum('ng,nge->ne', g_onehot, fine)
    top_v, top_i = lax.top_k(fine_sel, MOE_TOPK)
    w_top = p_g * jax.nn.softmax(top_v, axis=-1)
    expert_ids = gsel[:, None] * MOE_PER_GROUP + top_i
    combine = jnp.einsum('nk,nke->ne', w_top,
                         jax.nn.one_hot(expert_ids, N_EXPERTS, dtype=jnp.float32)).astype(xt.dtype)
    y = jnp.zeros_like(xt)
    for e in range(N_EXPERTS):
        he = jax.nn.silu(xt @ w_gate[e]) * (xt @ w_up[e])
        y = y + combine[:, e:e + 1] * (he @ w_down[e])
    return y.reshape(B, T, D)

def setup_inputs(seed: int = 0) -> dict:
    key = jax.random.key(seed)
    ks = iter(jax.random.split(key, 64))
    L, D, G = DEPTH, D_MODEL, GROUP_W

    def nrm(shape, scale):
        return scale * jax.random.normal(next(ks), shape, jnp.float32)

    def gain(shape):
        return 1.0 + nrm(shape, 0.02)

    def unif(shape, lo, hi):
        return jax.random.uniform(next(ks), shape, jnp.float32, minval=lo, maxval=hi)

    inputs = {
        "x": nrm((BATCH, SEQ, D), 1.0),
        "norm1_w": gain((L, D)),
        "w_in": nrm((L, D, D_IN), D ** -0.5),
        "hgrn_lb_logits": nrm((L, G), 0.5),
        "hgrn_norm_w": gain((L, G)),
        "s5_lambda_re": -0.5 + nrm((L, S5_GROUPS, S5_STATE), 0.01),
        "s5_lambda_im": jnp.pi * jnp.arange(S5_STATE, dtype=jnp.float32) + nrm((L, S5_GROUPS, S5_STATE), 0.01),
        "s5_log_dt": unif((L, S5_GROUPS), math.log(S5_DT_MIN), math.log(S5_DT_MAX)),
        "s5_b_re": nrm((L, S5_GROUPS, S5_STATE, S5_CH), (2 * S5_CH) ** -0.5),
        "s5_b_im": nrm((L, S5_GROUPS, S5_STATE, S5_CH), (2 * S5_CH) ** -0.5),
        "s5_c_re": nrm((L, S5_GROUPS, S5_CH, S5_STATE), S5_STATE ** -0.5),
        "s5_c_im": nrm((L, S5_GROUPS, S5_CH, S5_STATE), S5_STATE ** -0.5),
        "s5_d": nrm((L, G), 1.0),
        "s5_w_glu": nrm((L, G, 2 * G), G ** -0.5),
        "rwkv_mu": unif((L, RWKV_COLS), 0.0, 1.0),
        "rwkv_w0": unif((L, G), -6.0, 1.0),
        "rwkv_w2": nrm((L, RWKV_W_LORA, G), RWKV_W_LORA ** -0.5),
        "rwkv_a0": nrm((L, G), 0.1),
        "rwkv_a2": nrm((L, RWKV_A_LORA, G), RWKV_A_LORA ** -0.5),
        "rwkv_g2": nrm((L, RWKV_G_LORA, G), RWKV_G_LORA ** -0.5),
        "rwkv_k_k": 0.85 + nrm((L, G), 0.02),
        "rwkv_k_a": gain((L, G)),
        "rwkv_r_k": nrm((L, G), 0.1),
        "rwkv_v0": 1.0 + nrm((L - 1, G), 0.1),
        "rwkv_v1": nrm((L - 1, G, RWKV_V_LORA), G ** -0.5),
        "rwkv_v2": nrm((L - 1, RWKV_V_LORA, G), RWKV_V_LORA ** -0.5),
        "rwkv_ln_w": gain((L, G)),
        "rwkv_ln_b": nrm((L, G), 0.02),
        "lru_conv_w": nrm((L, LRU_CONV, G), LRU_CONV ** -0.5),
        "lru_conv_b": nrm((L, G), 0.02),
        "lru_wa": nrm((L, LRU_HEADS, LRU_HD, LRU_HD), LRU_HD ** -0.5),
        "lru_ba": nrm((L, G), 0.02),
        "lru_wx": nrm((L, LRU_HEADS, LRU_HD, LRU_HD), LRU_HD ** -0.5),
        "lru_bx": nrm((L, G), 0.02),
        "lru_lambda": None,
        "merge_gain": None,
    }
    a_lru = unif((L, G), 0.9, 0.999) ** (1.0 / LRU_C)
    inputs["lru_lambda"] = jnp.log(a_lru) - jnp.log1p(-a_lru)
    inputs["merge_gain"] = gain((L, D_MIX))
    inputs["w_out"] = nrm((L, D_MIX, D), D_MIX ** -0.5)
    inputs["norm2_w"] = gain((L, D))
    inputs["moe_coarse_w"] = nrm((L, D, MOE_GROUPS), D ** -0.5)
    inputs["moe_coarse_b"] = nrm((L, MOE_GROUPS), 0.01)
    inputs["moe_fine_w"] = nrm((L, MOE_GROUPS, D, MOE_PER_GROUP), D ** -0.5)
    inputs["moe_fine_b"] = nrm((L, MOE_GROUPS, MOE_PER_GROUP), 0.01)
    inputs["moe_w_gate"] = nrm((L, N_EXPERTS, D, D_EXPERT), D ** -0.5)
    inputs["moe_w_up"] = nrm((L, N_EXPERTS, D, D_EXPERT), D ** -0.5)
    inputs["moe_w_down"] = nrm((L, N_EXPERTS, D_EXPERT, D), D_EXPERT ** -0.5)
    inputs["final_norm_w"] = gain((D,))
    return inputs

def reference(x, norm1_w, w_in, hgrn_lb_logits, hgrn_norm_w, s5_lambda_re, s5_lambda_im, s5_log_dt,
              s5_b_re, s5_b_im, s5_c_re, s5_c_im, s5_d, s5_w_glu, rwkv_mu, rwkv_w0, rwkv_w2, rwkv_a0,
              rwkv_a2, rwkv_g2, rwkv_k_k, rwkv_k_a, rwkv_r_k, rwkv_v0, rwkv_v1, rwkv_v2, rwkv_ln_w,
              rwkv_ln_b, lru_conv_w, lru_conv_b, lru_wa, lru_ba, lru_wx, lru_bx, lru_lambda,
              merge_gain, w_out, norm2_w, moe_coarse_w, moe_coarse_b, moe_fine_w, moe_fine_b,
              moe_w_gate, moe_w_up, moe_w_down, final_norm_w):
    B, T, D = x.shape
    lb_all = jnp.cumsum(jax.nn.softmax(hgrn_lb_logits.astype(jnp.float32), axis=0), axis=0)
    lb_all = lb_all - lb_all[:1]
    h = x
    v_first = None
    for l in range(DEPTH):
        hn = rms_norm(h, norm1_w[l])
        proj = hn @ w_in[l]
        hq, hf, hi, hg, su, rw, lg, lx = jnp.split(proj, _splits(COL_SIZES), axis=-1)
        o_a = hgrn2_mixer(hq, hf, hi, hg, lb_all[l], hgrn_norm_w[l])
        o_b = s5_mixer(su, s5_lambda_re[l], s5_lambda_im[l], s5_log_dt[l], s5_b_re[l], s5_b_im[l],
                       s5_c_re[l], s5_c_im[l], s5_d[l], s5_w_glu[l])
        v_mix = None if l == 0 else (rwkv_v0[l - 1], rwkv_v1[l - 1], rwkv_v2[l - 1])
        o_c, v_first = rwkv7_mixer(rw, rwkv_mu[l], rwkv_w0[l], rwkv_w2[l], rwkv_a0[l], rwkv_a2[l],
                                   rwkv_g2[l], rwkv_k_k[l], rwkv_k_a[l], rwkv_r_k[l], rwkv_ln_w[l],
                                   rwkv_ln_b[l], v_first, v_mix)
        o_d = rglru_mixer(lg, lx, lru_conv_w[l], lru_conv_b[l], lru_wa[l], lru_ba[l], lru_wx[l],
                          lru_bx[l], lru_lambda[l])
        mix = jnp.concatenate([o_a, o_b, o_c, o_d], axis=-1).reshape(B, T, N_MIX_GROUPS, GROUP_W)
        mix = rms_norm(mix, merge_gain[l].reshape(N_MIX_GROUPS, GROUP_W)).reshape(B, T, D_MIX)
        h = h + mix @ w_out[l]
        h = h + hier_moe(rms_norm(h, norm2_w[l]), moe_coarse_w[l], moe_coarse_b[l], moe_fine_w[l],
                         moe_fine_b[l], moe_w_gate[l], moe_w_up[l], moe_w_down[l])
    return rms_norm(h, final_norm_w)


_drawn_inputs = setup_inputs


def setup_inputs(seed=0):
    import zlib

    import numpy as np

    out = dict(_drawn_inputs(seed))
    spreads = {}
    factors = {'hgrn_norm_w': 22.135,
     's5_lambda_re': 200.0,
     'rwkv_k_k': 24.715,
     'rwkv_k_a': 3.331,
     'rwkv_ln_w': 19.476,
     'rwkv_ln_b': 19.853,
     'lru_ba': 21.981,
     'lru_bx': 13.841,
     'merge_gain': 8.922,
     'moe_coarse_b': 24.833,
     'moe_fine_b': 16.87,
     'final_norm_w': 23.001,
     's5_lambda_im': 27.632,
     's5_log_dt': 29.12,
     's5_b_re': 38.592,
     's5_b_im': 34.616,
     's5_c_re': 40.56,
     's5_c_im': 35.656,
     'norm2_w': 5.879}
    for name, (base, spread) in spreads.items():
        noise = np.random.default_rng([zlib.crc32(name.encode()), seed]).standard_normal(out[name].shape)
        drawn = base * np.exp(spread * noise) if base else spread * noise
        out[name] = __import__('jax').numpy.asarray(drawn.astype(out[name].dtype))
    for name, factor in factors.items():
        out[name] = (out[name] * factor).astype(out[name].dtype)
    return out
```

```python
import math
from contextlib import ExitStack

import concourse.bass as bass
from concourse import mybir

F32 = mybir.dt.float32
I32 = mybir.dt.int32
U32 = mybir.dt.uint32
ALU = mybir.AluOpType
ACT = mybir.ActivationFunctionType
AX = mybir.AxisListType

P = 128
SEQ = 256
D_MODEL = 1024
DC = D_MODEL // P
GROUP_W = 256
NB = GROUP_W // P
TB = SEQ // P
HEAD = 64
RMS_EPS = 1e-6
GN_EPS = 64e-5

GROUPS = ["wag", "k", "r", "v", "su", "lx", "lg", "hf", "hq", "hi", "hg"]
FIRST_COLUMN = {"hq": 0, "hf": 256, "hi": 512, "hg": 768, "su": 1024, "r": 1280, "k": 1536, "v": 1792,
                "wag": 2048, "lg": 2304, "lx": 2560}

CH = 64
NCH = SEQ // CH
NM = NB * NCH
RW_C = math.exp(-0.5)
LEVELS = int(math.log2(CH))

HG_LEVELS = (128, 64, 32, 16, 8, 4, 2, 1)

S5_T = 8
S5_CH = 16

N_EXPERTS = 32
N_COARSE = 4
PER_GROUP = 8
D_EXPERT = 512
FC = D_EXPERT // P
SLOTS = 64
PAIRS = N_EXPERTS // 2
UNITS = 6
UNIT = 4096

TWO_PI = 2 * math.pi
TP1 = 6.28125
TP2 = 0.0019350051879882812
TP3 = TWO_PI - TP1 - TP2
MAGIC = 12582912.0

PARAMS = [("norm1", 8), ("w0", 2), ("a0", 2), ("k_k", 2), ("k_a", 2), ("r_k", 2), ("ln_w", 2),
          ("ln_b", 2), ("conv", 8), ("conv_b", 2), ("ba", 2), ("bx", 2), ("lam", 2), ("hnorm", 2),
          ("s5d", 2), ("gain", 8), ("mu", 8), ("lr", 8), ("li", 8), ("ldt", 8)]
PCOL = {}
NPAR = 0
for _n, _w in PARAMS:
    PCOL[_n] = (NPAR, _w)
    NPAR += _w
SMALL = [("wa2", 256), ("g2", 256), ("lwa", 128), ("lwx", 128), ("bre", 128),
         ("bim", 128), ("cre", 128), ("cim", 128)]
SCOL = {}
NSMALL = 0
for _n, _w in SMALL:
    SCOL[_n] = (NSMALL, _w)
    NSMALL += _w


def build_layer(nc, x, xT, params, small, glu, router, w_in, w_out, norm2_w, final_w, w_gate, w_up, w_down, out, dbg=None):
    with ExitStack() as ctx:
        def sb(name, shape, dt=F32):
            return ctx.enter_context(nc.sbuf_tensor(name, shape, dt))

        def sem(name):
            return ctx.enter_context(nc.semaphore(name))

        ring = sb("ring", [P, UNITS * UNIT])
        spread = sb("spread", [P, 8192])
        work = sb("work", [P, 18, 512])
        xs = sb("xs", [P, 2048])
        par = sb("par", [P, NPAR])
        sml = sb("sml", [P, NSMALL])
        pads = {n: sb("pad_" + n, [P, NB, SEQ + 1]) for n in ("wag", "k", "r", "v")}
        lxp = sb("lxp", [P, NB, SEQ + 3])
        kept = {n: sb("kept_" + n, [P, NB, SEQ]) for n in ("hf", "hq", "hi", "su", "lg", "hg")}
        kept["lx"] = lxp
        kept.update(pads)
        ident = sb("ident", [P, P])
        ones = sb("ones", [P, P])
        headsum = sb("headsum", [P, P])
        ident64 = sb("ident64", [P, CH])
        lev = sb("lev", [P, LEVELS, CH])
        m_strict = sb("m_strict", [P, CH])
        m_incl = sb("m_incl", [P, CH])
        xor_i = kept["hg"][:, 0, 0:2 * CH].rearrange("p (a b) -> p a b", a=2).bitcast(I32)
        xor_f = kept["hg"][:, 1, 0:CH]
        cst = sb("cst", [P, 8])
        state = sb("state", [P, 2, NB, CH])
        state_g = sb("state_g", [P, NB, CH])
        rhs_t = sb("rhs_t", [P, NB, CH])
        u_t = sb("u_t", [P, NB, CH])
        gend = sb("gend", [P, NM])
        rstd = sb("rstd", [P, SEQ])
        col = sb("col", [P, 64])
        s5c = sb("s5c", [P, 16, S5_T])
        prefix = kept["hq"][:, 0, 0:P]
        iota = kept["hq"][:, 1, 0:SLOTS]
        iota32 = kept["hq"][:, 1, SLOTS:SLOTS + N_EXPERTS]
        rout = kept["hi"][:, :, :].rearrange("p a b -> p (a b)")[:, 0:DC * 36 + 36]
        banks8 = ctx.enter_context(nc.psum_tensor("banks8", [P, 8, 512], F32))
        ps = [banks8[:, i, :] for i in range(8)]

        def w(i, n=1):
            return work[:, i:i + n, :].rearrange("p a b -> p (a b)")

        def w3(i):
            return work[:, i, :].rearrange("p (a b) -> p a b", a=NB)

        def pc(name, j=0):
            a, _ = PCOL[name]
            return par[:, a + j:a + j + 1]

        def pcs(name):
            a, n = PCOL[name]
            return par[:, a:a + n]

        def sc(name):
            a, n = SCOL[name]
            return sml[:, a:a + n]

        def flat(t):
            return t[:, :, :].rearrange("p a b -> p (a b)")

        def bc(ap, shape):
            return ap.broadcast_to(shape)

        s_x = sem("s_x")
        s_small = sem("s_small")
        s_win = [sem(f"s_win{i}") for i in range(11)]
        s_wout = sem("s_wout")
        s_xnat = sem("s_xnat")
        s_rows = sem("s_rows")
        s_out = sem("s_out")
        unit_full = [sem(f"unit_full{u}") for u in range(UNITS)]
        unit_free = [sem(f"unit_free{u}") for u in range(UNITS)]
        v_own = sem("v_own")
        a_own = sem("a_own")
        g_own = sem("g_own")
        consts = sem("consts")
        vconst = sem("vconst")
        sq_act = sem("sq_act")
        sq_dve = sem("sq_dve")
        ms_mm = sem("ms_mm")
        rstd1 = sem("rstd1")
        xn_ready = sem("xn_ready")
        proj_mm = sem("proj_mm")
        proj_kept = sem("proj_kept")
        wag_mixed = sem("wag_mixed")
        wag_act = sem("wag_act")
        lora_mm = sem("lora_mm")
        lora_act = sem("lora_act")
        rw_cum = sem("rw_cum")
        rw_exp = sem("rw_exp")
        kk_sq = sem("kk_sq")
        head_mm = sem("head_mm")
        kk_max = sem("kk_max")
        kk_inv = sem("kk_inv")
        rk_ready = sem("rk_ready")
        scaled = sem("scaled")
        score_mm = sem("score_mm")
        score_kept = sem("score_kept")
        nat_mm = sem("nat_mm")
        nat_kept = sem("nat_kept")
        lev_m = sem("lev_m")
        lev_p = sem("lev_p")
        lev_pk = sem("lev_pk")
        lev_x = sem("lev_x")
        lev_xk = sem("lev_xk")
        ch_rhs = sem("ch_rhs")
        ch_rhsk = sem("ch_rhsk")
        ch_u = sem("ch_u")
        ch_uk = sem("ch_uk")
        ch_s = sem("ch_s")
        ch_sk = sem("ch_sk")
        ch_y = sem("ch_y")
        y_kept = sem("y_kept")
        gn_mm = sem("gn_mm")
        gn_sq = sem("gn_sq")
        gn_rstd = sem("gn_rstd")
        hg_gates = sem("hg_gates")
        hg_f = sem("hg_f")
        hg_ln = sem("hg_ln")
        hg_diff = sem("hg_diff")
        hg_e = sem("hg_e")
        hg_scaled = sem("hg_scaled")
        hg_vt = sem("hg_vt")
        hg_vn = sem("hg_vn")
        hg_sc = sem("hg_sc")
        hg_sck = sem("hg_sck")
        hg_qk = sem("hg_qk")
        hg_qkmm = sem("hg_qkmm")
        hg_o = sem("hg_o")
        hg_osq = sem("hg_osq")
        hg_omm = sem("hg_omm")
        hg_orstd = sem("hg_orstd")
        s5_dt = sem("s5_dt")
        s5_th = sem("s5_th")
        s5_trig = sem("s5_trig")
        s5_b = sem("s5_b")
        s5_bt = sem("s5_bt")
        s5_bu = sem("s5_bu")
        s5_rot = sem("s5_rot")
        s5_x = sem("s5_x")
        s5_y = sem("s5_y")
        s5_pre = sem("s5_pre")
        s5_gelu = sem("s5_gelu")
        s5_glu = sem("s5_glu")
        s5_sig = sem("s5_sig")
        lr_sp = sem("lr_sp")
        lr_xc = sem("lr_xc")
        lr_coef = sem("lr_coef")
        lr_mm = sem("lr_mm")
        lr_gates = sem("lr_gates")
        lr_ln = sem("lr_ln")
        lr_sq = sem("lr_sq")
        lr_gelu = sem("lr_gelu")
        mg_sq = sem("mg_sq")
        mg_mm = sem("mg_mm")
        mg_rstd = sem("mg_rstd")
        mixed = sem("mixed")
        wo_mm = sem("wo_mm")
        h_ready = sem("h_ready")
        n2_ss = sem("n2_ss")
        n2_rstd = sem("n2_rstd")
        x2_ready = sem("x2_ready")
        x2t_mm = sem("x2t_mm")
        x2t_kept = sem("x2t_kept")
        logit_mm = sem("logit_mm")
        r_exp = sem("r_exp")
        r_expd = sem("r_expd")
        rank_mm = sem("rank_mm")
        routed = sem("routed")
        p_ready = sem("p_ready")
        pw_ready = sem("pw_ready")
        pw_half = sem("pw_half")
        gate_done, up_done, down_done = unit_free[1], unit_free[3], unit_free[5]
        gath_mm = sem("gath_mm")
        xg_kept = sem("xg_kept")
        silu_k = sem("silu_k")
        h_k = sem("h_k")
        pwt_mm = sem("pwt_mm")
        ht_mm = sem("ht_mm")
        pwt_k = sem("pwt_k")
        ht_k = sem("ht_k")
        y_k = sem("y_k")
        y_mm = sem("y_mm")
        ysum = sem("ysum")
        fin_ss = sem("fin_ss")
        fin_rstd = sem("fin_rstd")
        fin = sem("fin")
        dn_load = sem("dn_load")
        dn_own = sem("dn_own")
        dn_pe = sem("dn_pe")
        dn_act = sem("dn_act")
        dn_dve = sem("dn_dve")

        OUT_BANK = ((0, 1), (2, 5))
        LEVEL_BANK = (2, 6)

        def win(n):
            return ring[:, n * 2048:(n + 1) * 2048].rearrange("p (c j) -> p c j", c=DC)

        wo = spread[:, :].rearrange("p (c n) -> p c n", c=DC)
        xT_t = xs[:, :].rearrange("p (c t) -> p c t", c=DC)
        hN = xs[:, :].rearrange("p (b d) -> p b d", b=TB)
        cosT = spread[:, 0:2048].rearrange("p (j t) -> p j t", j=S5_T)
        sinT = spread[:, 2048:4096].rearrange("p (j t) -> p j t", j=S5_T)
        s5w = [spread[:, 4096 + 1024 * i:4096 + 1024 * (i + 1)].rearrange("p (j t) -> p j t", j=4) for i in range(4)]
        ang, angk = (spread[:, 6144 + 512 * i:6144 + 512 * (i + 1)].rearrange("p (r j n) -> p r j n", r=2, j=S5_T) for i in range(2))
        glu_w = xs[:, 0:1024].rearrange("p (b n) -> p b n", b=NB)
        bt_s5 = xs[:, 1024:1536].rearrange("p (k b n) -> p k b n", k=2, b=NB)
        s5_act = s5w[2].rearrange("p j t -> p (j t)")[:, 0:512].rearrange("p (b t) -> p b t", b=NB)
        s5_gate = s5w[3].rearrange("p j t -> p (j t)")[:, 0:512]
        bnat = [spread[:, 7680 + 256 * i:7680 + 256 * (i + 1)] for i in range(2)]
        cx = xs[:, 1536:2048].rearrange("p (k j c) -> p k j c", k=2, j=S5_T)
        mixT = [kept["hg"], kept["su"], pads["wag"], kept["lg"]]

        def mix_ap(n, b):
            t = mixT[n]
            return t[:, b, 1:SEQ + 1] if n == 2 else t[:, b, :]

        def mix3(n):
            t = mixT[n]
            return t[:, :, 1:SEQ + 1] if n == 2 else t[:, :, :]

        x2 = w(0, 4).rearrange("p (b d) -> p b d", b=TB)
        x2T = w(4, 4).rearrange("p (c t) -> p c t", c=DC)
        n2w = w(8, 2)
        fw = w(10, 2)
        lg = work[:, 12, 0:72].rearrange("p (b n) -> p b n", b=TB)
        rt = work[:, 13, :]
        selm = w(14)
        M = work[:, 14, 0:64].rearrange("p (b e) -> p b e", b=TB)
        C = work[:, 14, 64:128 + 4].rearrange("p (b e) -> p b e", b=TB)
        KEY = work[:, 14, 160:160 + 68].rearrange("p (b e) -> p b e", b=TB)
        CR = work[:, 14, 256:320].rearrange("p (b e) -> p b e", b=TB)
        M0 = work[:, 14, 320:384].rearrange("p (b e) -> p b e", b=TB)
        M1 = work[:, 14, 384:448].rearrange("p (b e) -> p b e", b=TB)
        flag_i = sb("flag_i", [1, 1], I32)
        xg = spread[:, 0:1024].rearrange("p (c s) -> p c s", c=DC)
        sg = spread[:, 1024:1536]
        hb = spread[:, 1536:2048]
        hT = spread[:, 2048:2560].rearrange("p (c s) -> p c s", c=FC)
        Yb = spread[:, 2560:3584]
        Pm = spread[:, 3584:3840].rearrange("p (b s) -> p b s", b=TB)
        PW = spread[:, 3840:4096].rearrange("p (b s) -> p b s", b=TB)
        PWT = spread[:, 4096:4352]
        junk = spread[:, 4352:5376]

        def unit_w(u, ab):
            return ring[:, u * UNIT + ab * 2048:u * UNIT + (ab + 1) * 2048]

        wg_d = w_gate.rearrange("e (p c) f -> e p (c f)", p=P)
        wu_d = w_up.rearrange("e (p c) f -> e p (c f)", p=P)
        wd_d = w_down.rearrange("e (p c) d -> e p (c d)", p=P)

        block = ctx.enter_context(nc.Block())

        @block.sync
        def _(sp):
            sp.dma_start(xs[:, :], xT).then_inc(s_x, 16)
            sp.dma_start(par[:, :], params).then_inc(s_x, 16)
            sp.dma_start(win(0), w_in[0]).then_inc(s_win[0], 16)
            sp.dma_start(sml[:, :], small).then_inc(s_small, 16)
            for n in range(1, 11):
                sp.dma_start(win(n), w_in[n]).then_inc(s_win[n], 16)

            def load_unit(u, e, first=False):
                for ab in range(2):
                    src = (wg_d, wg_d, wu_d, wu_d, wd_d, wd_d)[u]
                    sp.dma_start(unit_w(u, ab), src[e + ab, :, (u % 2) * 2048:(u % 2 + 1) * 2048]).then_inc(unit_full[u], 16)

            for u in range(UNITS):
                sp.wait_ge(proj_mm, min(2 * u + 2, 11))
                load_unit(u, 0)
            sp.dma_start(xs[:, 0:1024], glu).then_inc(s_xnat, 16)
            sp.wait_ge(s5_glu, 1)
            sp.dma_start(hN, x.rearrange("(b p) d -> p b d", p=P)).then_inc(s_xnat, 16)
            sp.wait_ge(mg_sq, 2)
            sp.dma_start(wo, w_out.rearrange("(c p) n -> p c n", p=P)).then_inc(s_wout, 16)
            sp.wait_ge(mixed, 4)
            sp.dma_start(rout, router).then_inc(s_rows, 16)
            sp.dma_start(n2w, norm2_w.partition_broadcast(P)).then_inc(s_rows, 16)
            sp.dma_start(fw, final_w.partition_broadcast(P)).then_inc(s_rows, 16)
            if dbg is not None:
                for n in range(4):
                    sp.dma_start(dbg[n], mix3(n)).then_inc(s_out, 16)
                sp.wait_ge(s_out, 64)
            with sp.Fori(1, PAIRS) as i:
                for u in range(UNITS):
                    sp.wait_ge(unit_free[u], i)
                    load_unit(u, 2 * i)
            sp.wait_ge(routed, 2)
            flag = sp.value_load(flag_i[0:1, 0:1], min_val=0, max_val=1)
            with sp.If(flag > 0):
                with sp.Fori(0, N_EXPERTS) as e:
                    sp.wait_ge(dn_pe, e * 6 + 1)
                    for k, src in enumerate((wg_d, wu_d, wd_d)):
                        sp.dma_start(ring[:, k * UNIT:(k + 1) * UNIT], src[e]).then_inc(dn_load, 16)
            with sp.Else():
                sp.nop()
            for b in range(TB):
                sp.wait_ge(fin, b + 1)
                sp.dma_start(out.rearrange("(b p) d -> b p d", p=P)[b], hN[:, b, :]).then_inc(s_out, 16)
            sp.wait_ge(s_out, 32 if dbg is None else 96)

        @block.gpsimd
        def _(pool):
            G = nc.gpsimd
            n = [0]

            def link(ins, s=None):
                n[0] += 1
                ins.then_inc(g_own, 1)
                pool.wait_ge(g_own, n[0])

            for t in ("wag", "k", "r", "v"):
                link(G.memset(pads[t][:, :, 0:1], 0.0))
            link(G.memset(lxp[:, :, 0:3], 0.0))
            link(G.memset(ones[:, :], 1.0))
            link(G.memset(headsum[:, :], 0.0))
            link(G.memset(headsum[0:64, 0:64], 1.0))
            link(G.memset(headsum[64:128, 64:128], 1.0))
            link(G.memset(cst[:, 0:1], RMS_EPS))
            link(G.memset(cst[:, 1:2], 10 * math.log(2.0)))
            link(G.memset(cst[:, 2:3], GN_EPS))
            link(G.memset(cst[:, 3:4], 1.0))
            G.memset(cst[:, 4:5], 0.0).then_inc(consts, 1)
            link(G.memset(ident[:, :], 0.0))
            G.affine_select(out=ident[:, :], in_=ident[:, :], compare_op=ALU.not_equal, fill=1.0, base=0,
                            pattern=[[-1, P]], channel_multiplier=1).then_inc(consts, 1)
            link(G.iota(xor_i[0:64, 0, :], pattern=[[0, CH]], base=0, channel_multiplier=1))
            link(G.iota(xor_i[64:128, 0, :], pattern=[[0, CH]], base=0, channel_multiplier=1))
            G.iota(xor_i[:, 1, :], pattern=[[1, CH]], base=0, channel_multiplier=0).then_inc(consts, 1)
            for r in range(2):
                link(G.iota(ang[:, r, :, 0:16], pattern=[[0, S5_T], [1, 16]], base=0, channel_multiplier=0,
                            allow_small_or_imprecise_dtypes=True))
                ins = G.iota(ang[:, r, :, 16:32], pattern=[[0, S5_T], [16, 16]], base=0, channel_multiplier=0,
                             allow_small_or_imprecise_dtypes=True)
                if r == 0:
                    link(ins)
            ins.then_inc(consts, 1)
            link(G.memset(bnat[0], 0.0))
            G.memset(bnat[1], 0.0).then_inc(consts, 1)
            pool.wait_ge(mixed, 4)
            link(G.memset(prefix, 1.0))
            link(G.affine_select(out=prefix, in_=prefix, compare_op=ALU.is_gt, fill=0.0, base=0,
                                 pattern=[[1, P]], channel_multiplier=-1))
            link(G.iota(iota, pattern=[[1, SLOTS]], base=0, channel_multiplier=0,
                        allow_small_or_imprecise_dtypes=True))
            G.iota(iota32, pattern=[[1, N_EXPERTS]], base=0, channel_multiplier=0,
                   allow_small_or_imprecise_dtypes=True).then_inc(consts, 1)

        @block.tensor
        def _(pe):
            mm = pe.matmul
            pe.wait_ge(consts, 1)
            for c in range(DC):
                pe.wait_ge((sq_act, sq_dve)[c // 4], 1)
                i = mm(ps[2][:, 0:SEQ], ones[:, :], w(c // 2)[:, (c % 2) * SEQ:(c % 2 + 1) * SEQ], start=c == 0, stop=c == DC - 1)
            i.then_inc(ms_mm, 1)
            for g in range(11):
                pe.wait_ge(s_win[g], 16)
                if g >= 2:
                    pe.wait_ge(proj_kept, g - 1)
                for b in range(NB):
                    for c in range(DC):
                        if g == 0 and b == 0:
                            pe.wait_ge(xn_ready, c + 1)
                        i = mm(ps[g % 2][:, b * SEQ:(b + 1) * SEQ], win(g)[:, c, b * P:(b + 1) * P],
                               xT_t[:, c, :], start=c == 0, stop=c == DC - 1)
                i.then_inc(proj_mm, 1)
                if g == 2:
                    pe.wait_ge(s_small, 16)
                    pe.wait_ge(wag_act, 2)
                    wa, g2 = sc("wa2"), sc("g2")
                    for b in range(NB):
                        mm(ps[2][:, b * SEQ:(b + 1) * SEQ], wa[0:64, b * P:(b + 1) * P], pads["wag"][0:64, 0, 1:SEQ + 1], start=True, stop=True)
                    for b in range(NB):
                        mm(ps[3][:, b * SEQ:(b + 1) * SEQ], wa[64:128, b * P:(b + 1) * P], pads["wag"][64:128, 0, 1:SEQ + 1], start=True, stop=True)
                    for b in range(NB):
                        i = mm(ps[4][:, b * SEQ:(b + 1) * SEQ], g2[:, b * P:(b + 1) * P], pads["wag"][:, 1, 1:SEQ + 1], start=True, stop=True)
                    i.then_inc(lora_mm, 1)
                    pe.wait_ge(kk_sq, 1)
                    mm(ps[5], headsum[:, :], w(8), start=True, stop=True).then_inc(head_mm, 1)
                if g == 4:
                    pe.wait_ge(rk_ready, 2)
                    mm(ps[6], headsum[:, :], w(4), start=True, stop=True).then_inc(head_mm, 1)
                if g == 7:
                    pe.wait_ge(lr_xc, 1)
                    pe.wait_ge(lora_act, 5)
                    pe.wait_ge(kk_max, 1)
                    for k, name in enumerate(("lwa", "lwx")):
                        wt = sc(name)
                        for bb in range(NB):
                            for h in range(2):
                                q = slice(64 * h, 64 * h + 64)
                                i = mm(ps[4 + k][q, bb * SEQ:(bb + 1) * SEQ], wt[q, bb * 64:(bb + 1) * 64], w3(7)[q, bb, :], start=True, stop=True)
                    i.then_inc(lr_mm, 1)

            def merge(n):
                pe.wait_ge(mg_sq, n + 1)
                if n >= 1:
                    pe.wait_ge(mg_rstd, n)
                for b in range(NB):
                    i = mm(ps[7][:, 0:SEQ], ones[:, :], w(17)[:, b * SEQ:(b + 1) * SEQ], start=b == 0, stop=b == NB - 1)
                i.then_inc(mg_mm, 1)

            def s5_inputs(half):
                for jj in range(4):
                    for k in range(2):
                        j = half * 4 + jj
                        r = slice(32 * jj, 32 * jj + 32)
                        i = mm(ps[(0, 1, 2, 7)[jj]][:, k * SEQ:(k + 1) * SEQ], bt_s5[r, k, j // 4, :],
                               kept["su"][r, j // 4, :], start=True, stop=True)
                i.then_inc(s5_bu, 1)

            def s5_outputs(half):
                pe.wait_ge(s5_x, half + 1)
                for jj in range(4):
                    j = half * 4 + jj
                    o = ps[6][32 * jj:32 * jj + 32, half * SEQ:(half + 1) * SEQ]
                    mm(o, cx[:, 0, j, :], s5w[0][:, jj, :], start=True, stop=False)
                    i = mm(o, cx[:, 1, j, :], s5w[1][:, jj, :], start=False, stop=True)
                i.then_inc(s5_y, 1)

            AR = w(0, 2).rearrange("p (m r t) -> p m r t", m=NM, r=2)
            pe.wait_ge(scaled, 1)
            pe.wait_ge(lr_gates, 4)
            for k, src in enumerate((w(2), w(3))):
                for m in range(NM):
                    for h in range(2):
                        r = slice(64 * h, 64 * h + 64)
                        i = mm(ps[2 + 2 * k + m // 4][r, (m % 4) * 128:(m % 4 + 1) * 128], src[r, m * CH:(m + 1) * CH],
                               AR[r, m, :, :].rearrange("p r t -> p (r t)"), start=True, stop=True)
                i.then_inc(score_mm, 1)
            pe.wait_ge(s5_b, 1)
            pe.wait_ge(consts, 2)
            pe.wait_ge(proj_kept, 11)
            for k in range(2):
                for b in range(NB):
                    i = pe.transpose(ps[0][:, (2 * k + b) * P:(2 * k + b + 1) * P], bnat[k][:, b * P:(b + 1) * P], ident[:, :])
            i.then_inc(s5_bu, 1)
            merge(0)
            pe.wait_ge(head_mm, 2)
            pe.wait_ge(rk_ready, 3)
            pe.wait_ge(mg_rstd, 1)
            pe.wait_ge(vconst, 1)
            banks = (6, 7, 2)
            for k in range(3):
                if k == 2:
                    pe.wait_ge(score_kept, 1)
                for m in range(NM):
                    for h in range(2):
                        r = slice(64 * h, 64 * h + 64)
                        b, c = m // NCH, m % NCH
                        src = pads["v"][r, b, 1 + c * CH:1 + (c + 1) * CH] if k == 0 else w(1 + k)[r, m * CH:(m + 1) * CH]
                        i = mm(ps[banks[k]][r, m * CH:(m + 1) * CH], src, ident64[r, :], start=True, stop=True)
                i.then_inc(nat_mm, 1)
            for l in range(LEVELS):
                pe.wait_ge(lev_m, l + 1)
                if l >= 1:
                    pe.wait_ge(lev_xk, 2 * l)
                if l == 0:
                    pe.wait_ge(score_kept, 4)
                for m in range(NM):
                    for h in range(2):
                        r = slice(64 * h, 64 * h + 64)
                        i = mm(ps[3][r, m * CH:(m + 1) * CH], w(14)[r, m * CH:(m + 1) * CH], w(11)[r, m * CH:(m + 1) * CH], start=True, stop=True)
                i.then_inc(lev_p, 1)
                if l == 0:
                    pe.wait_ge(s5_bt, 1)
                    pe.wait_ge(nat_kept, 3)
                    s5_inputs(0)
                if l == 3:
                    s5_outputs(0)
                    s5_inputs(1)
                pe.wait_ge(lev_pk, l + 1)
                if l < LEVELS - 1:
                    for m in range(NM):
                        for h in range(2):
                            r = slice(64 * h, 64 * h + 64)
                            i = mm(ps[4][r, m * CH:(m + 1) * CH], w(12)[r, m * CH:(m + 1) * CH], w(13)[r, m * CH:(m + 1) * CH], start=True, stop=True)
                    i.then_inc(lev_x, 1)
                for m in range(NM):
                    for h in range(2):
                        r = slice(64 * h, 64 * h + 64)
                        i = mm(ps[5][r, m * CH:(m + 1) * CH], w(13)[r, m * CH:(m + 1) * CH], w(12)[r, m * CH:(m + 1) * CH], start=True, stop=True)
                i.then_inc(lev_x, 1)
            s5_outputs(1)
            pe.wait_ge(lev_xk, 2 * LEVELS - 1)
            for c in range(NCH):
                if c >= 1:
                    pe.wait_ge(ch_sk, 2 * c)
                for b in range(NB):
                    m = b * NCH + c
                    for h in range(2):
                        r = slice(64 * h, 64 * h + 64)
                        o = ps[3][r, b * CH:(b + 1) * CH]
                        i = mm(o, w(8)[r, m * CH:(m + 1) * CH], w(4)[r, m * CH:(m + 1) * CH], start=True, stop=c == 0)
                        if c >= 1:
                            i = mm(o, AR[r, m, 0, :], state[r, c % 2, b, :], start=False, stop=True)
                i.then_inc(ch_rhs, 1)
                pe.wait_ge(ch_rhsk, c + 1)
                for b in range(NB):
                    m = b * NCH + c
                    for h in range(2):
                        r = slice(64 * h, 64 * h + 64)
                        i = mm(ps[4][r, b * CH:(b + 1) * CH], w(12)[r, m * CH:(m + 1) * CH], rhs_t[r, b, :], start=True, stop=True)
                i.then_inc(ch_u, 1)
                pe.wait_ge(ch_uk, c + 1)
                if c < NCH - 1:
                    for b in range(NB):
                        m = b * NCH + c
                        for h in range(2):
                            r = slice(64 * h, 64 * h + 64)
                            o = ps[5][r, b * CH:(b + 1) * CH]
                            mm(o, w(5)[r, m * CH:(m + 1) * CH], u_t[r, b, :], start=True, stop=False)
                            i = mm(o, w(6)[r, m * CH:(m + 1) * CH], w(4)[r, m * CH:(m + 1) * CH], start=False, stop=True)
                    i.then_inc(ch_s, 1)
                for b in range(NB):
                    m = b * NCH + c
                    for h in range(2):
                        r = slice(64 * h, 64 * h + 64)
                        o = ps[0][r, m * CH:(m + 1) * CH]
                        mm(o, u_t[r, b, :], w(9)[r, m * CH:(m + 1) * CH], start=True, stop=False)
                        i = mm(o, w(4)[r, m * CH:(m + 1) * CH], w(10)[r, m * CH:(m + 1) * CH], start=False, stop=c == 0)
                        if c >= 1:
                            i = mm(o, state[r, c % 2, b, :], AR[r, m, 1, :], start=False, stop=True)
                i.then_inc(ch_y, 1)
                if c == 0:
                    pe.wait_ge(s5_gelu, 1)
                    pe.wait_ge(s_xnat, 16)
                    for ob in range(4):
                        for b in range(NB):
                            i = mm(ps[1 + ob // 2][:, (ob % 2) * SEQ:(ob % 2 + 1) * SEQ], glu_w[:, b, ob * P:(ob + 1) * P],
                                   s5_act[:, b, :], start=b == 0, stop=b == NB - 1)
                    i.then_inc(s5_glu, 1)
                if c == 2:
                    merge(1)
            pe.wait_ge(y_kept, 1)
            mm(ps[4], headsum[:, :], w(17), start=True, stop=True).then_inc(gn_mm, 1)
            pe.wait_ge(gn_sq, 1)
            mm(ps[5], headsum[:, :], w(13), start=True, stop=True).then_inc(gn_mm, 1)


            def project_out(mixers, tb, n, first=False, last=False):
                for q in mixers:
                    for b in range(NB):
                        i = mm(ps[OUT_BANK[tb][n]], mix_ap(q, b)[:, tb * P:(tb + 1) * P], wo[:, 2 * q + b, n * 512:(n + 1) * 512],
                               start=first and q == mixers[0] and b == 0, stop=last and b == NB - 1)
                if last:
                    i.then_inc(wo_mm, 1)

            pe.wait_ge(hg_gates, 2)
            for b in range(NB):
                for tb in range(TB):
                    i = pe.transpose(ps[3][:, tb * 256 + b * P:tb * 256 + (b + 1) * P], kept["hi"][:, b, tb * P:(tb + 1) * P], ident[:, :])
            i.then_inc(hg_vt, 1)
            merge(2)
            pe.wait_ge(mixed, 2)
            pe.wait_ge(s_wout, 16)
            project_out((1, 3), 0, 0, first=True)
            for li, L in enumerate(HG_LEVELS):
                pe.wait_ge(hg_scaled, li + 1)
                if li == 2:
                    pe.wait_ge(hg_vn, 1)
                    pe.wait_ge(mg_rstd, 3)
                if li >= 4:
                    pe.wait_ge(hg_sck, li - 3)
                for hd in range(4):
                    e, b = hd % 2, hd // 2
                    r = slice(64 * e, 64 * e + 64)
                    t = w3(li)[r, b, :]
                    if L == 128:
                        i = mm(ps[4 + e][:, b * P:(b + 1) * P], t[:, 0:P], t[:, P:SEQ], start=True, stop=True)
                        continue
                    for hf in range(2):
                        if L == 64:
                            i = mm(ps[4 + e][0:64, 256 + (b * 2 + hf) * 64:256 + (b * 2 + hf + 1) * 64], t[:, hf * P:hf * P + 64],
                                   t[:, hf * P + 64:hf * P + 128], start=True, stop=True)
                            continue
                        for q in range(2):
                            ts_ = slice(hf * P + 64 * q, hf * P + 64 * q + 64)
                            i = mm(ps[LEVEL_BANK[li % 2] + e][64 * q:64 * q + 64, (b * 2 + hf) * 64:(b * 2 + hf + 1) * 64], t[:, ts_], t[:, ts_],
                                   start=True, stop=True)
                i.then_inc(hg_sc, 1)
                if li == 0:
                    project_out((1, 3), 0, 1, first=True)
                if li == 3:
                    pe.wait_ge(mixed, 3)
                    project_out((2,), 0, 0)
                if li == 5:
                    project_out((2,), 0, 1)
            pe.wait_ge(hg_qk, 1)
            pe.wait_ge(hg_sck, 5)
            mm(ps[3], headsum[:, :], flat(kept["hf"]), start=True, stop=True).then_inc(hg_qkmm, 1)
            pe.wait_ge(hg_sck, 7)
            vn = w(10).rearrange("p (t c) -> p t c", t=TB)
            SC = w(15, 2).rearrange("p (e b f t) -> p b e f t", e=2, b=NB, f=2)
            SX = w(13).rearrange("p (e b t) -> p b e t", e=2, b=NB)
            for hd in range(4):
                r = slice(64 * (hd % 2), 64 * (hd % 2) + 64)
                b = hd // 2
                cs = slice(hd * 64, hd * 64 + 64)
                mm(ps[6][r, b * SEQ:b * SEQ + P], vn[:, 0, cs], SC[:, b, hd % 2, 0, :], start=True, stop=True)
                mm(ps[6][r, b * SEQ + P:(b + 1) * SEQ], vn[:, 1, cs], SC[:, b, hd % 2, 1, :], start=True, stop=False)
                i = mm(ps[6][r, b * SEQ + P:(b + 1) * SEQ], vn[:, 0, cs], SX[:, b, hd % 2, :], start=False, stop=True)
            i.then_inc(hg_o, 1)
            project_out((1,), 1, 0, first=True)
            pe.wait_ge(hg_osq, 1)
            mm(ps[4], headsum[:, :], w(0), start=True, stop=True).then_inc(hg_omm, 1)
            project_out((2, 3), 1, 0)
            project_out((1,), 1, 1, first=True)
            merge(3)
            project_out((2, 3), 1, 1)
            pe.wait_ge(mixed, 4)
            for tb in range(TB):
                for n in range(2):
                    project_out((0,), tb, n, last=True)
            for tb in range(TB):
                pe.wait_ge(x2_ready, tb + 1)
                for c in range(DC):
                    i = pe.transpose(ps[2 * tb + c // 4][:, (c % 4) * P:(c % 4 + 1) * P], x2[:, tb, c * P:(c + 1) * P], ident[:, :])
                i.then_inc(x2t_mm, 1)
            pe.wait_ge(s_rows, 48)
            router = rout[:, 0:DC * 36].rearrange("p (c n) -> p c n", c=DC)
            for tb in range(TB):
                pe.wait_ge(x2t_kept, 2 * tb + 2)
                for c in range(DC):
                    i = mm(ps[6 + tb][:, 0:36], x2T[:, c, tb * P:(tb + 1) * P], router[:, c, :], start=c == 0, stop=c == DC - 1)
                i.then_inc(logit_mm, 1)
            pe.wait_ge(x2t_kept, 4)
            pe.wait_ge(y_k, 2)
            pe.wait_ge(pwt_k, 1)
            for k in range(4):
                mm(ps[k], PWT[:, 0:P], Yb[:, 0:512], start=True, stop=False, skip_group_check=True)
            pe.wait_ge(r_exp, 2)
            pe.wait_ge(consts, 6)
            mm(ps[4][:, 0:32], prefix, M[:, 0, :], start=True, stop=True)
            mm(ps[4][:, 32:64], prefix, M[:, 1, :], start=True, stop=False)
            mm(ps[4][:, 32:64], ones[:, :], M[:, 0, :], start=False, stop=True)
            mm(ps[4][:, 64:96], ones[:, :], M[:, 0, :], start=True, stop=False)
            mm(ps[4][:, 64:96], ones[:, :], M[:, 1, :], start=False, stop=True).then_inc(rank_mm, 1)

            gB, uB, d0, d1 = ps[4], ps[5], ps[6], ps[7]
            pe.wait_ge(routed, 2)

            def gather():
                for c in range(DC):
                    for tb in range(TB):
                        i = mm((d0, d1)[c // 4][:, (c % 4) * P:(c % 4 + 1) * P], x2[:, tb, c:D_MODEL:DC], Pm[:, tb, :],
                               start=tb == 0, stop=tb == TB - 1)
                i.then_inc(gath_mm, 1)

            def scatter():
                for tb in range(TB):
                    for n in range(2):
                        i = mm(ps[2 * tb + n], PWT[:, tb * P:(tb + 1) * P], Yb[:, n * 512:(n + 1) * 512],
                               start=False, stop=False, skip_group_check=True)
                i.then_inc(y_mm, 1)

            pe.wait_ge(p_ready, 1)
            gather()
            with pe.Fori(0, PAIRS) as i:
                def products(bank, u0):
                    for u in (u0, u0 + 1):
                        pe.wait_ge(unit_full[u], i * 32 + 32)
                        for cc in range(4):
                            c = (u - u0) * 4 + cc
                            for ab in range(2):
                                m_ = mm(bank[64 * ab:64 * ab + 64, :], xg[:, c, 64 * ab:64 * ab + 64],
                                        unit_w(u, ab)[:, cc * 512:(cc + 1) * 512], start=c == 0, stop=c == DC - 1)
                        m_.then_inc(unit_free[u], 1)

                pe.wait_ge(xg_kept, i * 2 + 2)
                pe.wait_ge(ht_k, i + 1)
                products(gB, 0)
                pe.wait_ge(y_k, i * 2 + 2)
                pe.wait_ge(pwt_k, i + 1)
                scatter()
                products(uB, 2)
                pe.wait_ge(p_ready, i + 2)
                gather()
                pe.wait_ge(h_k, i + 1)
                for c in range(FC):
                    m_ = pe.transpose(gB[:, c * P:(c + 1) * P], hb[:, c:D_EXPERT:FC], ident[:, :])
                m_.then_inc(ht_mm, 1)
                pe.wait_ge(pw_ready, i + 1)
                for tb in range(TB):
                    m_ = pe.transpose(uB[:, tb * P:(tb + 1) * P], PW[:, tb, :], ident[:, :])
                m_.then_inc(pwt_mm, 1)
                pe.wait_ge(ht_k, i + 2)
                pe.wait_ge(xg_kept, i * 2 + 4)
                for u in (4, 5):
                    pe.wait_ge(unit_full[u], i * 32 + 32)
                    for cc in range(2):
                        c = (u - 4) * 2 + cc
                        for n in range(2):
                            for ab in range(2):
                                m_ = mm((d0, d1)[n][64 * ab:64 * ab + 64, :], hT[:, c, 64 * ab:64 * ab + 64],
                                        unit_w(u, ab)[:, cc * 1024 + n * 512:cc * 1024 + (n + 1) * 512], start=c == 0, stop=c == FC - 1)
                    m_.then_inc(unit_free[u], 1)
            pe.wait_ge(y_k, 2 * PAIRS + 2)
            pe.wait_ge(pwt_k, PAIRS + 1)
            scatter()

            flag = pe.value_load(flag_i[0:1, 0:1], min_val=0, max_val=1)
            with pe.If(flag > 0):
                pe.wait_ge(ysum, 2)
                for tb in range(TB):
                    for c in range(DC):
                        i = pe.transpose(ps[2 * tb + c // 4][:, (c % 4) * P:(c % 4 + 1) * P], x2[:, tb, c:D_MODEL:DC], ident[:, :])
                i.then_inc(dn_pe, 1)
                pe.wait_ge(dn_dve, 1)
                with pe.Fori(0, N_EXPERTS) as e:
                    pe.wait_ge(dn_load, e * 48 + 48)
                    wgs = ring[:, 0:UNIT].rearrange("p (c f) -> p c f", c=DC)
                    wus = ring[:, UNIT:2 * UNIT].rearrange("p (c f) -> p c f", c=DC)
                    wds = ring[:, 2 * UNIT:3 * UNIT].rearrange("p (c d) -> p c d", c=FC)
                    for tb in range(TB):
                        for c in range(DC):
                            mm(gB[:, :], x2T[:, c, tb * P:(tb + 1) * P], wgs[:, c, :], start=c == 0, stop=c == DC - 1)
                        for c in range(DC):
                            m_ = mm(uB[:, :], x2T[:, c, tb * P:(tb + 1) * P], wus[:, c, :], start=c == 0, stop=c == DC - 1)
                        m_.then_inc(dn_pe, 1)
                        pe.wait_ge(dn_dve, e * 6 + 3 * tb + 2)
                        for c in range(FC):
                            m_ = pe.transpose(gB[:, c * P:(c + 1) * P], hb[:, c:D_EXPERT:FC], ident[:, :])
                        m_.then_inc(dn_pe, 1)
                        pe.wait_ge(dn_dve, e * 6 + 3 * tb + 3)
                        for n in range(2):
                            for c in range(FC):
                                m_ = mm((d0, d1)[n][:, :], hT[:, c, :], wds[:, c, n * 512:(n + 1) * 512], start=c == 0, stop=c == FC - 1)
                        m_.then_inc(dn_pe, 1)
                        pe.wait_ge(dn_dve, e * 6 + 3 * tb + 4)
            with pe.Else():
                pe.nop()

        @block.scalar
        def _(act):
            A = nc.scalar
            n_own = [0]

            def link(ins):
                n_own[0] += 1
                ins.then_inc(a_own, 1)
                act.wait_ge(a_own, n_own[0])

            act.wait_ge(consts, 1)
            act.wait_ge(s_x, 32)
            A.activation(w(0, 2), xs[:, 0:1024], ACT.Square).then_inc(sq_act, 1)

            def inv_sqrt(src, dst, eps_col, scale, ready):
                link(A.activation(dst, src, ACT.Ln, bias=cst[:, eps_col:eps_col + 1], scale=scale))
                A.activation(dst, dst, ACT.Exp, scale=-0.5).then_inc(ready, 1)

            act.wait_ge(ms_mm, 1)
            inv_sqrt(ps[2][:, 0:SEQ], rstd[:, :], 0, 1.0 / D_MODEL, rstd1)

            def keep(g):
                name = GROUPS[g]
                act.wait_ge(proj_mm, g + 1)
                src = ps[g % 2].rearrange("p (b t) -> p b t", b=NB)
                t = kept[name]
                off = {"wag": 1, "k": 1, "r": 1, "v": 1, "lx": 3}.get(name, 0)
                A.copy(t[:, :, off:off + SEQ], src).then_inc(proj_kept, 1)

            link(A.activation(col[:, 0:2], pcs("lam"), ACT.Exp, scale=-1.0))
            A.activation(s5c[:, 0, :], pcs("ldt"), ACT.Exp).then_inc(s5_dt, 1)
            act.wait_ge(s5_th, 1)
            A.activation(s5c[:, 1, :], s5c[:, 1, :], ACT.Exp).then_inc(s5_dt, 1)
            A.activation(col[:, 0:2], col[:, 0:2], ACT.Ln, bias=cst[:, 3:4]).then_inc(lr_sp, 1)
            keep(0)
            act.wait_ge(s5_th, 2)
            A.activation(ang, ang, ACT.Sin).then_inc(s5_trig, 1)
            keep(1)
            act.wait_ge(wag_mixed, 1)
            A.activation(pads["wag"][0:64, 0, 1:SEQ + 1], pads["wag"][0:64, 0, 1:SEQ + 1], ACT.Tanh).then_inc(wag_act, 1)
            A.activation(pads["wag"][:, 1, 1:SEQ + 1], pads["wag"][:, 1, 1:SEQ + 1], ACT.Sigmoid).then_inc(wag_act, 1)
            keep(2)
            act.wait_ge(lora_mm, 1)
            for b in range(NB):
                A.activation(w3(9)[:, b, :], ps[2][:, b * SEQ:(b + 1) * SEQ], ACT.Sigmoid, bias=pc("w0", b)).then_inc(lora_act, 1)
            for b in range(NB):
                A.activation(w3(10)[:, b, :], ps[3][:, b * SEQ:(b + 1) * SEQ], ACT.Sigmoid, bias=pc("a0", b)).then_inc(lora_act, 1)
            A.copy(w(15), ps[4]).then_inc(lora_act, 1)
            keep(3)
            keep(4)
            act.wait_ge(rw_cum, 1)
            A.activation(w(12), w(11), ACT.Exp, scale=-RW_C).then_inc(rw_exp, 1)
            A.activation(w(13), w(11), ACT.Exp, scale=RW_C).then_inc(rw_exp, 1)
            act.wait_ge(rw_cum, 2)
            A.activation(w(14), w(9), ACT.Exp, scale=-RW_C).then_inc(rw_exp, 1)
            act.wait_ge(kk_max, 1)
            link(A.activation(w(8), w(8), ACT.Ln, scale=2.0 ** 20))
            A.activation(w(8), w(8), ACT.Exp, scale=-0.5, bias=cst[:, 1:2]).then_inc(kk_inv, 1)
            keep(5)
            keep(6)
            keep(7)
            act.wait_ge(lr_mm, 1)
            for b in range(NB):
                A.activation(w3(8)[:, b, :], ps[4][:, b * SEQ:(b + 1) * SEQ], ACT.Sigmoid, bias=pc("ba", b)).then_inc(lr_gates, 1)
            for b in range(NB):
                A.activation(w3(9)[:, b, :], ps[5][:, b * SEQ:(b + 1) * SEQ], ACT.Sigmoid, bias=pc("bx", b)).then_inc(lr_gates, 1)
            act.wait_ge(lr_coef, 1)
            act.wait_ge(lr_gates, 4)
            for b in range(NB):
                A.activation(w3(10)[:, b, :], w3(8)[:, b, :], ACT.Tanh, scale=col[:, 2 + b:3 + b]).then_inc(lr_gates, 1)
            for b in range(NB):
                A.activation(w3(8)[:, b, :], w3(8)[:, b, :], ACT.Exp, scale=col[:, 4 + b:5 + b]).then_inc(lr_gates, 1)
            A.activation(kept["lg"][:, :, :], kept["lg"][:, :, :], ACT.Gelu_apprx_tanh).then_inc(lr_gelu, 1)
            keep(8)
            act.wait_ge(lr_ln, 1)
            link(A.activation(w(10), w(10), ACT.Ln))
            A.activation(w(10), w(10), ACT.Exp, scale=0.5).then_inc(lr_sq, 1)
            keep(9)
            keep(10)
            act.wait_ge(s5_bu, 1)
            A.copy(bt_s5.rearrange("p a b c -> p (a b c)"), ps[0]).then_inc(s5_bt, 1)

            def merge(n):
                act.wait_ge(mg_mm, n + 1)
                if n:
                    act.wait_ge(mixed, n)
                link(A.activation(rstd[:, :], ps[7][:, 0:SEQ], ACT.Ln, bias=cst[:, 0:1], scale=1.0 / GROUP_W))
                A.activation(rstd[:, :], rstd[:, :], ACT.Exp, scale=-0.5).then_inc(mg_rstd, 1)

            merge(0)
            for k in range(3):
                act.wait_ge(nat_mm, k + 1)
                A.copy(w(4 + k), ps[(6, 7, 2)[k]]).then_inc(nat_kept, 1)
            for l in range(LEVELS):
                act.wait_ge(lev_p, l + 1)
                A.copy(w(13), ps[3]).then_inc(lev_pk, 1)
            act.wait_ge(s5_pre, 1)
            A.activation(s5_act, s5_act, ACT.Gelu_apprx_tanh).then_inc(s5_gelu, 1)
            for name in ("hq", "hi", "hg"):
                A.activation(flat(kept[name]), flat(kept[name]), ACT.Silu).then_inc(hg_gates, 1)
            A.activation(w(2), flat(kept["hf"]), ACT.Sigmoid).then_inc(hg_gates, 1)
            A.activation(flat(kept["hf"]), flat(kept["hf"]), ACT.Sigmoid, scale=-1.0).then_inc(hg_gates, 1)
            act.wait_ge(s5_glu, 1)
            A.activation(s5_gate, ps[2], ACT.Sigmoid).then_inc(s5_sig, 1)
            merge(1)
            act.wait_ge(hg_f, 1)
            A.activation(w(2), w(2), ACT.Ln).then_inc(hg_ln, 1)
            act.wait_ge(ch_y, NCH)
            A.copy(w(17), ps[0]).then_inc(y_kept, 1)
            act.wait_ge(gn_mm, 2)
            link(A.activation(w(14), ps[5], ACT.Ln, bias=cst[:, 2:3], scale=1.0 / HEAD))
            A.activation(w(14), w(14), ACT.Exp, scale=-0.5).then_inc(gn_rstd, 1)

            act.wait_ge(hg_vt, 1)
            A.copy(w(10), ps[3]).then_inc(hg_vn, 1)
            for k, L in enumerate(HG_LEVELS):
                if k == 1:
                    merge(2)
                act.wait_ge(hg_diff, k + 1)
                d = w((8, 12)[k % 2]).rearrange("p (n two l) -> p n two l", two=2, l=L)
                A.activation(d[:, :, 0, :], d[:, :, 0, :], ACT.Exp, scale=-1.0).then_inc(hg_e, 1)
                A.activation(d[:, :, 1, :], d[:, :, 1, :], ACT.Exp).then_inc(hg_e, 1)
            act.wait_ge(hg_omm, 1)
            link(A.activation(w(0), ps[4], ACT.Ln, bias=cst[:, 0:1], scale=1.0 / HEAD))
            A.activation(w(0), w(0), ACT.Exp, scale=-0.5).then_inc(hg_orstd, 1)
            merge(3)
            for tb in range(TB):
                act.wait_ge(h_ready, 2 * tb + 2)
                A.activation(w(14 + 2 * tb, 2), hN[:, tb, :], ACT.Square, accum_out=col[:, 8 + tb:9 + tb]).then_inc(n2_ss, 1)
            act.wait_ge(n2_ss, 2)
            link(A.activation(col[:, 10:12], col[:, 8:10], ACT.Ln, bias=cst[:, 0:1], scale=1.0 / D_MODEL))
            A.activation(col[:, 10:12], col[:, 10:12], ACT.Exp, scale=-0.5).then_inc(n2_rstd, 1)
            for tb in range(TB):
                act.wait_ge(x2t_mm, tb + 1)
                for q in range(2):
                    A.copy(x2T[:, 4 * q:4 * q + 4, tb * P:(tb + 1) * P], ps[2 * tb + q].rearrange("p (c t) -> p c t", c=4)).then_inc(x2t_kept, 1)
            act.wait_ge(r_exp, 1)
            A.activation(work[:, 12, 80:96].rearrange("p (b n) -> p b n", b=TB), work[:, 12, 96:112].rearrange("p (b n) -> p b n", b=TB), ACT.Exp).then_inc(r_expd, 1)
            act.wait_ge(gath_mm, 1)

            def keep_xg():
                for q in range(2):
                    A.copy(xg[:, 4 * q:4 * q + 4, :].rearrange("p c s -> p (c s)"), ps[6 + q]).then_inc(xg_kept, 1)

            keep_xg()
            with act.Fori(0, PAIRS) as i:
                act.wait_ge(gate_done, i + 1)
                A.activation(sg, ps[4], ACT.Silu).then_inc(silu_k, 1)
                act.wait_ge(gath_mm, i + 2)
                keep_xg()
                act.wait_ge(down_done, i + 1)
                A.copy(Yb[:, 0:512], ps[6]).then_inc(y_k, 1)
                A.copy(Yb[:, 512:1024], ps[7]).then_inc(y_k, 1)
            flag = act.value_load(flag_i[0:1, 0:1], min_val=0, max_val=1)
            with act.If(flag > 0):
                with act.Fori(0, N_EXPERTS) as e:
                    for tb in range(TB):
                        act.wait_ge(dn_pe, e * 6 + 3 * tb + 2)
                        A.activation(sg, ps[4], ACT.Silu).then_inc(dn_act, 1)
            with act.Else():
                act.nop()
            for tb in range(TB):
                act.wait_ge(fin_ss, tb + 1)
                link(A.activation(col[:, 14 + tb:15 + tb], col[:, 12 + tb:13 + tb], ACT.Ln, bias=cst[:, 0:1], scale=1.0 / D_MODEL))
                A.activation(col[:, 14 + tb:15 + tb], col[:, 14 + tb:15 + tb], ACT.Exp, scale=-0.5).then_inc(fin_rstd, 1)

        @block.vector
        def _(dve):
            V = nc.vector
            tt, ts, stt = V.tensor_tensor, V.tensor_scalar, V.scalar_tensor_tensor
            MUL, ADD, SUB = ALU.mult, ALU.add, ALU.subtract
            count = {}

            def link(ins, s=v_own):
                count[id(s)] = count.get(id(s), 0) + 1
                ins.then_inc(s, 1)
                dve.wait_ge(s, count[id(s)])

            dve.wait_ge(s_x, 32)
            link(tt(w(2, 2), xs[:, 1024:2048], xs[:, 1024:2048], MUL), sq_dve)
            dve.wait_ge(rstd1, 1)
            for c in range(DC):
                link(stt(xT_t[:, c, :], xT_t[:, c, :], pc("norm1", c), rstd[:, :], MUL, MUL), xn_ready)

            dve.wait_ge(s5_dt, 1)
            lr, li = pcs("lr"), pcs("li")
            link(tt(s5c[:, 1, :], lr, s5c[:, 0, :], MUL), s5_th)
            th, kf = s5c[:, 2, :], s5c[:, 3, :]
            link(tt(th, li, s5c[:, 0, :], MUL))

            def reduce_angle(a, k):
                link(ts(k, a, 1.0 / TWO_PI, MAGIC, MUL, ADD))
                link(ts(k, k, -MAGIC, None, ADD))
                for part in (TP1, TP2, TP3):
                    link(stt(a, k, -part, a, MUL, ADD))

            reduce_angle(th, kf)
            dve.wait_ge(consts, 4)
            for r in range(2):
                link(tt(ang[:, r, :, :], ang[:, r, :, :], th.unsqueeze(2).broadcast_to([P, S5_T, 32]), MUL))
            link(ts(ang[:, 1, :, :], ang[:, 1, :, :], math.pi / 2, None, ADD))
            af = ang.rearrange("p r j n -> p (r j n)")
            reduce_angle(af, angk.rearrange("p r j n -> p (r j n)"))
            link(ts(af, af, 3.141592, -3.141592, ALU.min, ALU.max), s5_th)
            def shift_mix(name, mu):
                t = pads[name]
                link(tt(w3(17), t[:, :, 0:SEQ], t[:, :, 1:SEQ + 1], SUB))
                for b in range(NB):
                    ins = stt(t[:, b, 1:SEQ + 1], w3(17)[:, b, :], pc("mu", mu + b), t[:, b, 1:SEQ + 1], MUL, ADD)
                    link(ins, wag_mixed if name == "wag" and b == 1 else v_own)

            def cumulate(dst, src, length, s=v_own):
                n = src.shape[1] // length
                for k in range(n):
                    t = slice(k * length, (k + 1) * length)
                    link(V.tensor_tensor_scan(dst[:, t], cst[:, 3:4].broadcast_to([P, length]), src[:, t], 0.0, MUL, ADD),
                         s if k == n - 1 else v_own)

            dve.wait_ge(proj_kept, 1)
            shift_mix("wag", 6)
            dve.wait_ge(consts, 3)
            link(V.tensor_copy(lev[:, 0:2, :], xor_i))
            link(tt(m_strict[:, :], lev[:, 0, :], lev[:, 1, :], ALU.is_lt))
            link(tt(m_incl[:, :], lev[:, 0, :], lev[:, 1, :], ALU.is_le))
            link(tt(xor_i[:, 0, :], xor_i[:, 0, :], xor_i[:, 1, :], ALU.bitwise_xor))
            link(V.tensor_copy(xor_f, xor_i[:, 0, :]))
            link(ts(ident64[:, :], xor_f, 0.0, None, ALU.is_equal))
            for l in range(LEVELS):
                link(ts(state[:, 0, 0, :], xor_f, float(2 ** (l + 1)), None, ALU.is_lt))
                link(stt(lev[:, l, :], xor_f, float(2 ** l), state[:, 0, 0, :], ALU.is_ge, MUL))
            link(tt(lev[:, :, :], lev[:, :, :], m_strict[:, :].unsqueeze(1).broadcast_to([P, LEVELS, CH]), MUL), vconst)

            k3, r3, v3 = (pads[n][:, :, 1:SEQ + 1] for n in ("k", "r", "v"))
            dve.wait_ge(proj_kept, 2)
            shift_mix("k", 2)
            for b in range(NB):
                link(ts(w3(7)[:, b, :], k3[:, b, :], pc("k_k", b), None, MUL))
            link(tt(w(8), w(7), w(7), MUL), kk_sq)
            dve.wait_ge(proj_kept, 3)
            shift_mix("r", 0)
            dve.wait_ge(lora_act, 2)
            cumulate(w(11), w(9), CH, rw_cum)
            link(tt(w(9), w(11), w(9), SUB), rw_cum)
            dve.wait_ge(lora_act, 4)
            for b in range(NB):
                link(ts(w3(5)[:, b, :], w3(10)[:, b, :], -1.0, pc("k_a", b), ADD, MUL))
            link(stt(w3(5), w3(5), 1.0, k3, ADD, MUL))
            for b in range(NB):
                link(stt(w3(4)[:, b, :], r3[:, b, :], pc("r_k", b), w3(5)[:, b, :], MUL, MUL), rk_ready)
            dve.wait_ge(head_mm, 1)
            link(ts(w(8), ps[5], 1e-24, None, ALU.max), kk_max)
            dve.wait_ge(proj_kept, 4)
            shift_mix("v", 4)
            dve.wait_ge(kk_inv, 1)
            link(tt(w(7), w(7), w(8), MUL))
            link(tt(w(6), w(7), w(10), MUL))
            AR = w(0, 2).rearrange("p (m r t) -> p m r t", m=NM, r=2)

            def by_chunk(t):
                return t.rearrange("p (m t) -> p m t", m=NM)

            dve.wait_ge(rw_exp, 3)
            link(stt(AR[:, :, 0, :], by_chunk(w(7)), -1.0, by_chunk(w(14)), MUL, MUL))
            for b in range(NB):
                link(tt(AR[:, b * NCH:(b + 1) * NCH, 1, :], r3[:, b, :].rearrange("p (c t) -> p c t", t=CH),
                        w3(12)[:, b, :].rearrange("p (c t) -> p c t", t=CH), MUL))
            link(V.tensor_copy(gend[:, :], by_chunk(w(12))[:, :, CH - 1]))
            link(tt(w(2), w(6), w(13), MUL))
            link(tt(w(3), w(5), w(13), MUL), scaled)
            dve.wait_ge(head_mm, 2)
            link(tt(w3(16), ps[6].rearrange("p (b t) -> p b t", b=NB), v3, MUL), rk_ready)
            def merge_square(k):
                link(tt(w3(17), mix3(k), mix3(k), MUL), mg_sq)

            def merge_scale(n, k):
                dve.wait_ge(mg_rstd, n + 1)
                for b in range(NB):
                    link(stt(mix_ap(k, b), mix_ap(k, b), pc("gain", 2 * k + b), rstd[:, :], MUL, MUL), mixed if b else v_own)

            dve.wait_ge(proj_kept, 6)
            dve.wait_ge(head_mm, 2)
            for b in range(NB):
                link(ts(w3(7)[:, b, :], lxp[:, b, 0:SEQ], pc("conv", b), pc("conv_b", b), MUL, ADD))
            for j in range(1, 4):
                for b in range(NB):
                    link(stt(w3(7)[:, b, :], lxp[:, b, j:j + SEQ], pc("conv", 2 * j + b), w3(7)[:, b, :], MUL, ADD),
                         lr_xc if (j, b) == (3, 1) else v_own)
            dve.wait_ge(lr_sp, 1)
            link(ts(col[:, 2:4], col[:, 0:2], 8.0, None, MUL))
            link(ts(col[:, 4:6], col[:, 0:2], -8.0, None, MUL), lr_coef)
            dve.wait_ge(s5_trig, 1)
            sn, cs = ang[:, 0, :, :], ang[:, 1, :, :]

            def outer(hi, lo):
                return (hi[:, :, 16:32].unsqueeze(3).broadcast_to([P, S5_T, 16, 16]),
                        lo[:, :, 0:16].unsqueeze(2).broadcast_to([P, S5_T, 16, 16]))

            c4, s4 = (t.rearrange("p j (a b) -> p j a b", a=16) for t in (cosT, sinT))
            tmp = spread[:, 4096:6144].rearrange("p (j a b) -> p j a b", j=S5_T, a=16)
            link(tt(c4, *outer(cs, cs), MUL))
            link(tt(tmp, *outer(sn, sn), MUL))
            link(tt(cosT, cosT, tmp.rearrange("p j a b -> p j (a b)"), SUB))
            link(tt(s4, *outer(sn, cs), MUL))
            link(tt(tmp, *outer(cs, sn), MUL))
            link(tt(sinT, sinT, tmp.rearrange("p j a b -> p j (a b)"), ADD))
            dve.wait_ge(lr_gates, 6)
            link(ts(w(10), w(10), 1e-18, None, ALU.max))
            link(ts(w(13), w(10), 1.0, None, ADD))
            link(V.reciprocal(w(13), w(13)))
            link(stt(w(10), w(10), 2.0, w(13), MUL, MUL), lr_ln)
            link(tt(w(9), w(9), w(7), MUL))
            dve.wait_ge(s5_dt, 2)
            S = [s5c[:, k, :] for k in range(16)]
            link(tt(S[4], S[1], cs[:, :, 1], MUL))
            link(ts(S[4], S[4], -1.0, None, ADD))
            link(tt(S[5], S[1], sn[:, :, 1], MUL))
            link(tt(S[6], lr, lr, MUL))
            link(tt(S[7], li, li, MUL))
            link(tt(S[6], S[6], S[7], ADD))
            link(V.reciprocal(S[7], S[6]))
            link(tt(S[8], S[4], lr, MUL))
            link(tt(S[9], S[5], li, MUL))
            link(tt(S[8], S[8], S[9], ADD))
            link(tt(S[8], S[8], S[7], MUL))
            link(tt(S[9], S[5], lr, MUL))
            link(tt(S[10], S[4], li, MUL))
            link(tt(S[9], S[9], S[10], SUB))
            link(tt(S[9], S[9], S[7], MUL))
            dve.wait_ge(s_small, 16)
            dve.wait_ge(consts, 5)

            def by_tile(name):
                return sc(name).rearrange("p (j c) -> p j c", j=S5_T)

            t1 = angk[:, 0, :, 0:16]
            t2 = angk[:, 1, :, 0:16]
            for k, (p1, p2, op) in enumerate((("bre", "bim", SUB), ("bim", "bre", ADD))):
                link(tt(t1, by_tile(p1), S[8].unsqueeze(2).broadcast_to([P, S5_T, 16]), MUL))
                link(tt(t2, by_tile(p2), S[9].unsqueeze(2).broadcast_to([P, S5_T, 16]), MUL))
                dst = bnat[k].rearrange("p (j c) -> p j c", j=S5_T)
                for h in range(2):
                    r = slice(64 * h, 64 * h + 64)
                    link(tt(dst[r, :, 16 * h:16 * h + 16], t1[r], t2[r], op))
            dve.wait_ge(lr_gates, 8)
            link(V.memset(w3(8)[:, 1, 0:1], 0.0))
            dve.wait_ge(lr_sq, 1)
            link(tt(w(13), w(9), w(10), MUL))
            link(V.tensor_tensor_scan(w(14), w(8), w(13), 0.0, MUL, ADD))
            dve.wait_ge(lr_gelu, 1)
            link(tt(flat(kept["lg"]), flat(kept["lg"]), w(14), MUL))
            merge_square(3)

            dve.wait_ge(proj_kept, 11)
            link(V.memset(cx, 0.0))
            for h in range(2):
                r = slice(64 * h, 64 * h + 64)
                link(V.tensor_copy(cx[r, 0, :, 16 * h:16 * h + 16], by_tile("cre")[r]))
                link(ts(cx[r, 1, :, 16 * h:16 * h + 16], by_tile("cim")[r], -1.0, None, MUL), s5_b if h else v_own)
            for k in range(2):
                dve.wait_ge(score_mm, k + 1)
                for q in range(2):
                    src = ps[2 + 2 * k + q].rearrange("p (m r t) -> p m r t", m=4, r=2)
                    ms = slice(4 * q, 4 * q + 4)
                    link(tt(by_chunk(w(7 + k))[:, ms, :], src[:, :, 0, :], m_strict[:, :].unsqueeze(1).broadcast_to([P, 4, CH]), MUL))
                    link(tt(by_chunk(w(9 + k))[:, ms, :], src[:, :, 1, :], m_incl[:, :].unsqueeze(1).broadcast_to([P, 4, CH]), MUL), score_kept)
            def s5_states(half, part):
                j0 = half * 4
                C4, S4 = cosT[:, j0:j0 + 4, :], sinT[:, j0:j0 + 4, :]
                if part == 0:
                    dve.wait_ge(s5_bu, half + 2)
                    if half:
                        dve.wait_ge(s5_y, 1)
                    for jj in range(4):
                        bank = ps[(0, 1, 2, 7)[jj]]
                        for out_k, in_k, tab_ in ((0, 0, C4), (2, 1, S4), (1, 1, C4), (3, 0, S4)):
                            ins = tt(s5w[out_k][:, jj, :], bank[:, in_k * SEQ:(in_k + 1) * SEQ], tab_[:, jj, :], MUL)
                            link(ins, s5_rot if (jj, out_k) == (3, 3) else v_own)
                    link(tt(s5w[0], s5w[0], s5w[2], ADD))
                    link(tt(s5w[1], s5w[1], s5w[3], SUB))
                if part == 1:
                    for jj in range(4):
                        mag = s5c[:, 1, j0 + jj:j0 + jj + 1].broadcast_to([P, SEQ])
                        link(V.tensor_tensor_scan(s5w[2][:, jj, :], mag, s5w[0][:, jj, :], 0.0, MUL, ADD))
                        link(V.tensor_tensor_scan(s5w[3][:, jj, :], mag, s5w[1][:, jj, :], 0.0, MUL, ADD))
                    link(tt(s5w[0], s5w[2], C4, MUL))
                    link(tt(s5w[1], s5w[2], S4, MUL))
                if part == 2:
                    link(tt(s5w[2], s5w[3], S4, MUL))
                    link(tt(s5w[0], s5w[0], s5w[2], SUB))
                    link(tt(s5w[3], s5w[3], C4, MUL))
                    link(tt(s5w[1], s5w[1], s5w[3], ADD), s5_x)

            link(V.tensor_copy(by_chunk(w(11)), ident64[:, :].unsqueeze(1).broadcast_to([P, NM, CH])))
            link(V.tensor_copy(by_chunk(w(12)), ident64[:, :].unsqueeze(1).broadcast_to([P, NM, CH])))
            for l in range(LEVELS):
                link(tt(by_chunk(w(14)), by_chunk(w(7)), lev[:, l, :].unsqueeze(1).broadcast_to([P, NM, CH]), MUL), lev_m)
                if l == 0:
                    merge_scale(0, 3)
                s5_states(l // 3, l % 3)
                if l < LEVELS - 1:
                    dve.wait_ge(lev_x, 2 * l + 1)
                    link(tt(w(11), ps[4], w(11), ADD), lev_xk)
                    dve.wait_ge(lev_x, 2 * l + 2)
                else:
                    dve.wait_ge(lev_x, 2 * l + 1)
                link(tt(w(12), ps[5], w(12), ADD), lev_xk)
            dve.wait_ge(s5_y, 2)
            for b in range(NB):
                link(stt(s5_act[:, b, :], kept["su"][:, b, :], pc("s5d", b), ps[6][:, b * SEQ:(b + 1) * SEQ], MUL, ADD),
                     s5_pre if b else v_own)
            gend3 = gend[:, :].rearrange("p (b c) -> p b c", b=NB)
            for c in range(NCH):
                if 1 <= c < NCH - 1:
                    for b in range(NB):
                        link(ts(state_g[:, b, :], state[:, c % 2, b, :], gend3[:, b, c:c + 1], None, MUL))
                dve.wait_ge(ch_rhs, c + 1)
                link(V.tensor_copy(rhs_t[:, :, :].rearrange("p b t -> p (b t)"), ps[3][:, 0:P]), ch_rhsk)
                dve.wait_ge(ch_u, c + 1)
                link(V.tensor_copy(u_t[:, :, :].rearrange("p b t -> p (b t)"), ps[4][:, 0:P]), ch_uk)
                if c < NCH - 1:
                    dve.wait_ge(ch_s, c + 1)
                    for b in range(NB):
                        nxt, src, g = state[:, (c + 1) % 2, b, :], ps[5][:, b * CH:(b + 1) * CH], gend3[:, b, c:c + 1]
                        link(ts(nxt, src, g, None, MUL) if c == 0 else stt(nxt, src, g, state_g[:, b, :], MUL, ADD), ch_sk)
                if c == 1:
                    dve.wait_ge(s5_sig, 1)
                    link(tt(flat(kept["su"]), ps[1], s5_gate, MUL))
                    merge_square(1)
                if c == 2:
                    dve.wait_ge(hg_gates, 4)
                    link(ts(w(2), w(2), 1e-18, None, ALU.max), hg_f)
            merge_scale(1, 1)

            hq, hf, hi, hg = (flat(kept[n]) for n in ("hq", "hf", "hi", "hg"))
            lam = w(11)

            def level_diff(k):
                L = HG_LEVELS[k]
                n = 512 // (2 * L)
                dk = w((8, 12)[k % 2])
                d, lp = (t.rearrange("p (n two l) -> p n two l", two=2, l=L) for t in (dk, lam))
                mid = lp[:, :, 0, L - 1:L]
                if L == 128:
                    link(tt(d[:, :, 0, :], lp[:, :, 0, :], mid.broadcast_to([P, n, L]), SUB))
                    link(V.tensor_copy(d[:, :, 1, :], lp[:, :, 1, :]), hg_diff)
                else:
                    link(tt(dk.rearrange("p (n l) -> p n l", l=2 * L), lam.rearrange("p (n l) -> p n l", l=2 * L),
                            mid.broadcast_to([P, n, 2 * L]), SUB), hg_diff)

            def level_scaled(k):
                L = HG_LEVELS[k]
                d, t, kk, qq = (t.rearrange("p (n two l) -> p n two l", two=2, l=L) for t in (w((8, 12)[k % 2]), w(k), hf, hq))
                dve.wait_ge(hg_e, 2 * k + 2)
                link(tt(t[:, :, 0, :], kk[:, :, 0, :], d[:, :, 0, :], MUL))
                link(tt(t[:, :, 1, :], qq[:, :, 1, :], d[:, :, 1, :], MUL), hg_scaled)

            acc, one = (w(k).rearrange("p (e n t) -> p e n t", e=2, n=4) for k in (14, 9))

            def level_masked(li):
                dve.wait_ge(hg_sc, li + 1)
                lb = LEVEL_BANK[li % 2]
                src = banks8[:, lb:lb + 2, 0:256].rearrange("p e (n t) -> p e n t", n=4)
                mask = lev[:, LEVELS + 1 - li, :].unsqueeze(1).unsqueeze(1).broadcast_to([P, 2, 4, CH])
                link(tt(one if li > 2 else acc, src, mask, MUL), hg_sck)
                if li > 2:
                    link(tt(w(14), w(14), w(9), ADD))

            dve.wait_ge(hg_ln, 1)
            cumulate(lam, w(2), P)
            dve.wait_ge(gn_mm, 1)
            link(stt(w(17), ps[4], -1.0 / HEAD, w(17), MUL, ADD))
            link(tt(w(13), w(17), w(17), MUL), gn_sq)
            level_diff(0)
            level_diff(1)
            dve.wait_ge(gn_rstd, 1)
            link(tt(w(17), w(17), w(14), MUL))
            for b in range(NB):
                link(ts(w3(17)[:, b, :], w3(17)[:, b, :], pc("ln_w", b), pc("ln_b", b), MUL, ADD))
            link(tt(w(17), w(17), w(16), ADD))
            link(tt(mix3(2), w3(17), w3(15), MUL))

            merge_square(2)

            dve.wait_ge(hg_gates, 5)
            level_scaled(0)
            level_diff(2)
            level_scaled(1)
            level_diff(3)
            merge_scale(2, 2)
            link(V.memset(w(15, 2), 0.0))
            for k in range(2, len(HG_LEVELS)):
                level_scaled(k)
                if k + 2 < len(HG_LEVELS):
                    level_diff(k + 2)
                if k > 2:
                    level_masked(k - 1)
            link(tt(hf, hf, hq, MUL), hg_qk)
            level_masked(len(HG_LEVELS) - 1)
            SC = w(15, 2).rearrange("p (e n t) -> p e n t", e=2, n=4)
            link(V.tensor_copy(SC[0:64, :, :, 0:64], acc[0:64]))
            link(V.tensor_copy(SC[64:128, :, :, 64:128], acc[64:128]))
            link(V.tensor_copy(SC[0:64, :, :, 64:128], banks8[0:64, 4:6, 256:512].rearrange("p e (n t) -> p e n t", n=4)))
            link(V.tensor_copy(w(13).rearrange("p (e t) -> p e t", e=2), banks8[:, 4:6, 0:SEQ]), hg_sck)
            dve.wait_ge(hg_qkmm, 1)
            link(tt(w(2), ps[3], hi, MUL))
            dve.wait_ge(hg_o, 1)
            link(tt(w(1), ps[6], w(2), ADD))
            link(tt(w(0), w(1), w(1), MUL), hg_osq)
            dve.wait_ge(hg_orstd, 1)
            link(tt(w(1), w(1), w(0), MUL))
            for b in range(NB):
                link(stt(kept["hg"][:, b, :], w3(1)[:, b, :], pc("hnorm", b), kept["hg"][:, b, :], MUL, MUL))
            merge_square(0)
            merge_scale(3, 0)

            dve.wait_ge(s_xnat, 32)
            for tb in range(TB):
                for n in range(2):
                    dve.wait_ge(wo_mm, 2 * tb + n + 1)
                    part = hN[:, tb, n * 512:(n + 1) * 512]
                    link(tt(part, ps[OUT_BANK[tb][n]], part, ADD), h_ready)
            link(V.memset(Yb[:, 0:512], 0.0), y_k)
            link(V.memset(Yb[:, 512:1024], 0.0), y_k)
            link(V.memset(PWT, 0.0), pwt_k)
            link(V.memset(hT, 0.0), ht_k)
            dve.wait_ge(n2_rstd, 1)
            dve.wait_ge(s_rows, 48)
            dve.wait_ge(consts, 6)
            for tb in range(TB):
                link(stt(x2[:, tb, :], hN[:, tb, :], col[:, 10 + tb:11 + tb], n2w, MUL, MUL), x2_ready)

            cz = rt[:, 0:16].rearrange("p (b n) -> p b n", b=TB)
            mx = rt[:, 16:32].rearrange("p (b n) -> p b n", b=TB)
            ix = rt[:, 32:48].rearrange("p (b n) -> p b n", b=TB)
            ixu = ix.bitcast(U32)
            fs = rt[:, 48:64].rearrange("p (b n) -> p b n", b=TB)
            fmx = rt[:, 64:80].rearrange("p (b n) -> p b n", b=TB)
            fix = rt[:, 80:96].rearrange("p (b n) -> p b n", b=TB)
            fixu = fix.bitcast(U32)
            gs = rt[:, 96:98]
            oh = rt[:, 100:108].rearrange("p (b n) -> p b n", b=TB)
            fi = rt[:, 108:112].rearrange("p (b n) -> p b n", b=TB)
            g8 = rt[:, 112:114]
            sm = rt[:, 114:116]
            w0_, w1_ = rt[:, 116:118], rt[:, 118:120]
            df = work[:, 12, 96:112].rearrange("p (b n) -> p b n", b=TB)
            ex = work[:, 12, 80:96].rearrange("p (b n) -> p b n", b=TB)
            link(V.memset(rt[:, 0:16], -3e38))
            link(V.memset(work[:, 12, 96:112], 0.0))
            for tb in range(TB):
                dve.wait_ge(logit_mm, tb + 1)
                link(tt(lg[:, tb, :], ps[6 + tb][:, 0:36], rout[:, DC * 36:], ADD))
                link(V.tensor_copy(cz[:, tb, 0:4], lg[:, tb, 0:4]))
                link(V.max(mx[:, tb, :], cz[:, tb, :]))
                link(V.max_index(ixu[:, tb, :], mx[:, tb, :], cz[:, tb, :]))
                link(V.tensor_copy(gs[:, tb:tb + 1], ixu[:, tb, 0:1]))
                link(ts(oh[:, tb, :], iota32[:, 0:4], gs[:, tb:tb + 1], None, ALU.is_equal))
                link(ts(fs[:, tb, :], lg[:, tb, 4:12], oh[:, tb, 0:1], None, MUL))
                for g in range(1, N_COARSE):
                    link(stt(fs[:, tb, :], lg[:, tb, 4 + 8 * g:12 + 8 * g], oh[:, tb, g:g + 1], fs[:, tb, :], MUL, ADD))
                link(V.max(fmx[:, tb, :], fs[:, tb, :]))
                link(V.max_index(fixu[:, tb, :], fmx[:, tb, :], fs[:, tb, :]))
                link(V.tensor_copy(fi[:, tb, :], fixu[:, tb, 0:2]))
                link(ts(df[:, tb, 0:4], cz[:, tb, 0:4], mx[:, tb, 0:1], None, SUB))
                link(tt(df[:, tb, 4:5], fmx[:, tb, 1:2], fmx[:, tb, 0:1], SUB), r_exp if tb else v_own)
            link(ts(g8, gs, float(PER_GROUP), None, MUL))
            for tb in range(TB):
                link(ts(fi[:, tb, :], fi[:, tb, :], g8[:, tb:tb + 1], None, ADD))
                link(ts(M0[:, tb, :], iota32, fi[:, tb, 0:1], None, ALU.is_equal))
                link(ts(M1[:, tb, :], iota32, fi[:, tb, 1:2], None, ALU.is_equal))
            link(tt(M, M0, M1, ADD), r_exp)
            dve.wait_ge(r_expd, 1)
            for tb in range(TB):
                link(V.tensor_reduce(sm[:, tb:tb + 1], ex[:, tb, 0:4], AX.X, ADD))
                link(ts(w1_[:, tb:tb + 1], ex[:, tb, 4:5], 1.0, None, ADD))
            link(tt(sm, sm, w1_, MUL))
            link(V.reciprocal(w0_, sm))
            for tb in range(TB):
                link(tt(w1_[:, tb:tb + 1], w0_[:, tb:tb + 1], ex[:, tb, 4:5], MUL))
            link(V.memset(C[:, :, 32:34], 0.0))
            link(V.memset(KEY[:, :, 32:34], -1.0))
            for tb in range(TB):
                link(ts(C[:, tb, 0:32], M0[:, tb, :], w0_[:, tb:tb + 1], None, MUL))
                link(stt(C[:, tb, 0:32], M1[:, tb, :], w1_[:, tb:tb + 1], C[:, tb, 0:32], MUL, ADD))
            dve.wait_ge(rank_mm, 1)
            rank = ps[4][:, 0:64].rearrange("p (b e) -> p b e", b=TB)
            link(stt(KEY[:, :, 0:32], rank, 1.0, M, ADD, MUL))
            link(ts(KEY[:, :, 0:32], KEY[:, :, 0:32], -1.0, None, ADD), routed)
            iota4 = iota.unsqueeze(1).unsqueeze(1).broadcast_to([P, TB, 2, SLOTS])

            def one_hot(dst, i):
                return tt(dst.rearrange("p b (a s) -> p b a s", a=2), iota4,
                          KEY[:, :, bass.ds(i, 2)].unsqueeze(3).broadcast_to([P, TB, 2, SLOTS]), ALU.is_equal)

            link(one_hot(Pm, 0), p_ready)
            link(stt(CR, rank, float(SLOTS), C[:, :, 0:32], ALU.is_ge, MUL))
            link(V.tensor_reduce(col[0:1, 20:21], ps[4][0:1, 64:96], AX.X, ALU.max))
            link(ts(flag_i[0:1, 0:1], col[0:1, 20:21], float(SLOTS), None, ALU.is_gt), routed)

            with dve.Fori(0, PAIRS) as i:
                dve.wait_ge(gath_mm, i + 1)
                one_hot(Pm, i * 2 + 2).then_inc(p_ready, 1)
                dve.wait_ge(gate_done, i + 1)
                one_hot(PW, i * 2).then_inc(pw_half, 1)
                dve.wait_ge(pw_half, i + 1)
                tt(PW.rearrange("p b (a s) -> p b a s", a=2), PW.rearrange("p b (a s) -> p b a s", a=2),
                   C[:, :, bass.ds(i * 2, 2)].unsqueeze(3).broadcast_to([P, TB, 2, SLOTS]), MUL).then_inc(pw_ready, 1)
                dve.wait_ge(silu_k, i + 1)
                dve.wait_ge(up_done, i + 1)
                tt(hb, ps[5], sg, MUL).then_inc(h_k, 1)
                dve.wait_ge(ht_mm, i + 1)
                V.tensor_copy(hT.rearrange("p c s -> p (c s)"), ps[4]).then_inc(ht_k, 1)
                dve.wait_ge(pwt_mm, i + 1)
                V.tensor_copy(PWT, ps[5][:, 0:256]).then_inc(pwt_k, 1)
            dve.wait_ge(y_mm, PAIRS + 1)
            for tb in range(TB):
                for n in range(2):
                    part = hN[:, tb, n * 512:(n + 1) * 512]
                    link(tt(part, ps[2 * tb + n], part, ADD), ysum if n else v_own)
            flag = dve.value_load(flag_i[0:1, 0:1], min_val=0, max_val=1)
            with dve.If(flag > 0):
                dve.wait_ge(dn_pe, 1)
                for tb in range(TB):
                    for q in range(2):
                        ins = V.tensor_copy(x2T[:, 4 * q:4 * q + 4, tb * P:(tb + 1) * P], ps[2 * tb + q].rearrange("p (c t) -> p c t", c=4))
                ins.then_inc(dn_dve, 1)
                with dve.Fori(0, N_EXPERTS) as e:
                    for tb in range(TB):
                        dve.wait_ge(dn_act, e * 2 + tb + 1)
                        tt(hb, ps[5], sg, MUL).then_inc(dn_own, 1)
                        dve.wait_ge(dn_own, e * 2 + tb + 1)
                        ts(hb, hb, CR[:, tb, bass.ds(e, 1)], None, MUL).then_inc(dn_dve, 1)
                        dve.wait_ge(dn_pe, e * 6 + 3 * tb + 3)
                        V.tensor_copy(hT.rearrange("p c s -> p (c s)"), ps[4]).then_inc(dn_dve, 1)
                        dve.wait_ge(dn_pe, e * 6 + 3 * tb + 4)
                        tt(hN[:, tb, 0:512], ps[6], hN[:, tb, 0:512], ADD)
                        tt(hN[:, tb, 512:1024], ps[7], hN[:, tb, 512:1024], ADD).then_inc(dn_dve, 1)
                dve.wait_ge(dn_dve, 6 * N_EXPERTS + 1)
            with dve.Else():
                dve.nop()
            for tb in range(TB):
                link(tt(junk, hN[:, tb, :], hN[:, tb, :], MUL))
                link(V.tensor_reduce(col[:, 12 + tb:13 + tb], junk, AX.X, ADD), fin_ss)
                dve.wait_ge(fin_rstd, tb + 1)
                link(stt(hN[:, tb, :], hN[:, tb, :], col[:, 14 + tb:15 + tb], fw, MUL, MUL), fin)


def kernel(**inputs):
    import numpy as np
    import concourse.bacc as bacc
    from concourse.bass_utils import run_bass_kernel_spmd

    a = {k: np.asarray(v) for k, v in inputs.items()}

    def columns(v, width=P):
        return v.reshape(-1, width).T

    state_cols = lambda v: v.reshape(S5_T, P).T
    params = {
        "norm1": columns(a["norm1_w"][0]), "w0": columns(a["rwkv_w0"][0]), "a0": columns(a["rwkv_a0"][0]),
        "k_k": columns(a["rwkv_k_k"][0]), "k_a": columns(a["rwkv_k_a"][0]), "r_k": columns(a["rwkv_r_k"][0]),
        "ln_w": columns(a["rwkv_ln_w"][0]), "ln_b": columns(a["rwkv_ln_b"][0]),
        "conv": columns(a["lru_conv_w"][0].reshape(-1)), "conv_b": columns(a["lru_conv_b"][0]),
        "ba": columns(a["lru_ba"][0]), "bx": columns(a["lru_bx"][0]), "lam": columns(a["lru_lambda"][0]),
        "hnorm": columns(a["hgrn_norm_w"][0]), "s5d": columns(a["s5_d"][0]), "gain": columns(a["merge_gain"][0]),
        "mu": columns(a["rwkv_mu"][0]), "lr": state_cols(a["s5_lambda_re"][0]), "li": state_cols(a["s5_lambda_im"][0]),
        "ldt": state_cols(np.repeat(a["s5_log_dt"][0], 64)),
    }
    router = np.concatenate([a["moe_coarse_w"][0], a["moe_fine_w"][0].transpose(1, 0, 2).reshape(D_MODEL, 32)], axis=1)
    rbias = np.concatenate([a["moe_coarse_b"][0], a["moe_fine_b"][0].reshape(-1)])

    def s5_b(v):
        return v.reshape(S5_T, P, S5_CH).transpose(1, 0, 2).reshape(P, -1)

    def heads(v):
        return v.reshape(NB, P, HEAD).transpose(1, 0, 2).reshape(P, -1)

    small = {
        "wa2": np.concatenate([a["rwkv_w2"][0], a["rwkv_a2"][0]]), "g2": a["rwkv_g2"][0],
        "lwa": heads(a["lru_wa"][0]), "lwx": heads(a["lru_wx"][0]),
        "bre": s5_b(a["s5_b_re"][0]), "bim": s5_b(a["s5_b_im"][0]),
        "cre": s5_b(a["s5_c_re"][0].transpose(0, 2, 1)), "cim": s5_b(a["s5_c_im"][0].transpose(0, 2, 1)),
    }
    w_in = a["w_in"][0]
    pieces = [w_in[:, FIRST_COLUMN[g]:FIRST_COLUMN[g] + 256].reshape(DC, P, 256).transpose(1, 0, 2) for g in GROUPS]
    arrays = {
        "x": a["x"][0],
        "xT": a["x"][0].T.reshape(DC, P, SEQ).transpose(1, 0, 2).reshape(P, -1),
        "params": np.concatenate([params[n] for n, _ in PARAMS], axis=1),
        "small": np.concatenate([small[n] for n, _ in SMALL], axis=1),
        "glu": a["s5_w_glu"][0].reshape(NB, P, 512).transpose(1, 0, 2).reshape(P, -1),
        "router": np.concatenate([router.reshape(DC, P, 36).transpose(1, 0, 2).reshape(P, -1), np.broadcast_to(rbias, (P, 36))], axis=1),
        "w_in": np.stack(pieces),
        "w_out": a["w_out"][0], "norm2_w": a["norm2_w"][0], "final_w": a["final_norm_w"],
        "w_gate": a["moe_w_gate"][0], "w_up": a["moe_w_up"][0], "w_down": a["moe_w_down"][0],
    }
    nc = bacc.Bacc("TRN2", target_bir_lowering=False, num_devices=1)
    feed, args = {}, []
    for name, v in arrays.items():
        v = np.ascontiguousarray(v)
        feed[f"in_{name}"] = v
        args.append(nc.dram_tensor(f"in_{name}", v.shape, mybir.dt.from_np(v.dtype), kind="ExternalInput").ap())
    out = nc.dram_tensor("out_0", (SEQ, D_MODEL), F32, kind="ExternalOutput").ap()
    build_layer(nc, *args, out)
    r = run_bass_kernel_spmd(nc, [feed], core_ids=[0])
    return np.asarray(r.results[0]["out_0"]).reshape(1, SEQ, D_MODEL)
```

```python
import math
from contextlib import ExitStack

import concourse.bass as bass
from concourse import mybir

F32 = mybir.dt.float32
I32 = mybir.dt.int32
U32 = mybir.dt.uint32
ALU = mybir.AluOpType
ACT = mybir.ActivationFunctionType
AX = mybir.AxisListType

P = 128
SEQ = 256
D_MODEL = 1024
DC = D_MODEL // P
GROUP_W = 256
NB = GROUP_W // P
TB = SEQ // P
HEAD = 64
RMS_EPS = 1e-6
GN_EPS = 64e-5

GROUPS = ["wag", "k", "r", "v", "su", "lx", "lg", "hf", "hq", "hi", "hg"]
FIRST_COLUMN = {"hq": 0, "hf": 256, "hi": 512, "hg": 768, "su": 1024, "r": 1280, "k": 1536, "v": 1792,
                "wag": 2048, "lg": 2304, "lx": 2560}

CH = 64
NCH = SEQ // CH
NM = NB * NCH
RW_C = math.exp(-0.5)
LEVELS = int(math.log2(CH))

HG_LEVELS = (128, 64, 32, 16, 8, 4, 2, 1)

S5_T = 8
S5_CH = 16

N_EXPERTS = 32
N_COARSE = 4
PER_GROUP = 8
D_EXPERT = 512
FC = D_EXPERT // P
SLOTS = 64
PAIRS = N_EXPERTS // 2
UNITS = 6
UNIT = 4096

TWO_PI = 2 * math.pi
TP1 = 6.28125
TP2 = 0.0019350051879882812
TP3 = TWO_PI - TP1 - TP2
MAGIC = 12582912.0

PARAMS = [("norm1", 8), ("w0", 2), ("a0", 2), ("k_k", 2), ("k_a", 2), ("r_k", 2), ("ln_w", 2),
          ("ln_b", 2), ("conv", 8), ("conv_b", 2), ("ba", 2), ("bx", 2), ("lam", 2), ("hnorm", 2),
          ("s5d", 2), ("gain", 8), ("mu", 8), ("lr", 8), ("li", 8), ("ldt", 8)]
PCOL = {}
NPAR = 0
for _n, _w in PARAMS:
    PCOL[_n] = (NPAR, _w)
    NPAR += _w
SMALL = [("wa2", 256), ("g2", 256), ("lwa", 128), ("lwx", 128), ("bre", 128),
         ("bim", 128), ("cre", 128), ("cim", 128)]
SCOL = {}
NSMALL = 0
for _n, _w in SMALL:
    SCOL[_n] = (NSMALL, _w)
    NSMALL += _w


def build_layer(nc, x, xT, params, small, glu, router, w_in, w_out, norm2_w, final_w, w_gate, w_up, w_down, out):
    with ExitStack() as ctx:
        def sb(name, shape, dt=F32):
            return ctx.enter_context(nc.sbuf_tensor(name, shape, dt))

        def sem(name):
            return ctx.enter_context(nc.semaphore(name))

        ring = sb("ring", [P, UNITS * UNIT])
        spread = sb("spread", [P, 8192])
        work = sb("work", [P, 18, 512])
        xs = sb("xs", [P, 2048])
        par = sb("par", [P, NPAR])
        sml = sb("sml", [P, NSMALL])
        early = sb("early", [P, 4 * NB * (SEQ + 1) + 4 * NB * SEQ])
        pads = {n: early[:, i * NB * (SEQ + 1):(i + 1) * NB * (SEQ + 1)].rearrange("p (b t) -> p b t", b=NB)
                for i, n in enumerate(("wag", "k", "r", "v"))}
        lxp = sb("lxp", [P, NB, SEQ + 3])
        kept = {n: sb("kept_" + n, [P, NB, SEQ])[:, :, :] for n in ("hq", "hi")}
        for i, n in enumerate(("hf", "su", "lg", "hg")):
            o = 4 * NB * (SEQ + 1) + i * NB * SEQ
            kept[n] = early[:, o:o + NB * SEQ].rearrange("p (b t) -> p b t", b=NB)
        kept["lx"] = lxp
        kept.update(pads)
        ident = sb("ident", [P, P])
        ones = sb("ones", [P, P])
        headsum = sb("headsum", [P, P])
        ident64 = sb("ident64", [P, CH])
        lev = sb("lev", [P, LEVELS, CH])
        m_strict = sb("m_strict", [P, CH])
        m_incl = sb("m_incl", [P, CH])
        xor_i = kept["hg"][:, 0, 0:2 * CH].rearrange("p (a b) -> p a b", a=2).bitcast(I32)
        xor_f = kept["hg"][:, 1, 0:CH]
        cst = sb("cst", [P, 8])
        state = sb("state", [P, 2, NB, CH])
        state_g = sb("state_g", [P, NB, CH])
        rhs_t = sb("rhs_t", [P, NB, CH])
        u_t = sb("u_t", [P, NB, CH])
        gend = sb("gend", [P, NM])
        rstd = sb("rstd", [P, SEQ])
        col = sb("col", [P, 64])
        s5c = sb("s5c", [P, 16, S5_T])
        prefix = kept["hq"][:, 0, 0:P]
        iota = kept["hq"][:, 1, 0:SLOTS]
        iota32 = kept["hq"][:, 1, SLOTS:SLOTS + N_EXPERTS]
        rout = kept["hi"][:, :, :].rearrange("p a b -> p (a b)")[:, 0:DC * 36 + 36]
        banks8 = ctx.enter_context(nc.psum_tensor("banks8", [P, 8, 512], F32))
        ps = [banks8[:, i, :] for i in range(8)]

        def w(i, n=1):
            return work[:, i:i + n, :].rearrange("p a b -> p (a b)")

        def w3(i):
            return work[:, i, :].rearrange("p (a b) -> p a b", a=NB)

        def pc(name, j=0):
            a, _ = PCOL[name]
            return par[:, a + j:a + j + 1]

        def pcs(name):
            a, n = PCOL[name]
            return par[:, a:a + n]

        def sc(name):
            a, n = SCOL[name]
            return sml[:, a:a + n]

        def flat(t):
            return t[:, :, :].rearrange("p a b -> p (a b)")

        def bc(ap, shape):
            return ap.broadcast_to(shape)

        s_x = sem("s_x")
        s_x0 = sem("s_x0")
        s_small = sem("s_small")
        s_win = [sem(f"s_win{i}") for i in range(11)]
        s_wout = sem("s_wout")
        s_xnat = sem("s_xnat")
        s_rows = sem("s_rows")
        s_out = sem("s_out")
        unit_full = [sem(f"unit_full{u}") for u in range(UNITS)]
        extra_full = [sem(f"extra_full{u}") for u in range(2)]
        unit_free = [sem(f"unit_free{u}") for u in range(UNITS)]
        v_own = sem("v_own")
        a_own = sem("a_own")
        g_own = sem("g_own")
        consts = sem("consts")
        vconst = sem("vconst")
        sq_act = sem("sq_act")
        sq_dve = sem("sq_dve")
        ms_mm = sem("ms_mm")
        rstd1 = sem("rstd1")
        xn_ready = sem("xn_ready")
        proj_mm = sem("proj_mm")
        proj_kept = sem("proj_kept")
        wag_mixed = sem("wag_mixed")
        wag_act = sem("wag_act")
        lora_mm = sem("lora_mm")
        lora_act = sem("lora_act")
        rw_cum = sem("rw_cum")
        rw_exp = sem("rw_exp")
        kk_sq = sem("kk_sq")
        head_mm = sem("head_mm")
        kk_max = sem("kk_max")
        kk_inv = sem("kk_inv")
        rk_ready = sem("rk_ready")
        scaled = sem("scaled")
        score_mm = sem("score_mm")
        score_kept = sem("score_kept")
        nat_mm = sem("nat_mm")
        nat_kept = sem("nat_kept")
        lev_m = sem("lev_m")
        lev_p = sem("lev_p")
        lev_pk = sem("lev_pk")
        lev_x = sem("lev_x")
        lev_xk = sem("lev_xk")
        ch_rhs = sem("ch_rhs")
        ch_rhsk = sem("ch_rhsk")
        ch_u = sem("ch_u")
        ch_uk = sem("ch_uk")
        ch_s = sem("ch_s")
        ch_sk = sem("ch_sk")
        ch_y = sem("ch_y")
        y_kept = sem("y_kept")
        gn_mm = sem("gn_mm")
        gn_sq = sem("gn_sq")
        gn_rstd = sem("gn_rstd")
        hg_gates = sem("hg_gates")
        hg_f = sem("hg_f")
        hg_ln = sem("hg_ln")
        hg_diff = sem("hg_diff")
        hg_e = sem("hg_e")
        hg_scaled = sem("hg_scaled")
        hg_vt = sem("hg_vt")
        hg_vn = sem("hg_vn")
        hg_sc = sem("hg_sc")
        hg_sck = sem("hg_sck")
        hg_qk = sem("hg_qk")
        hg_qkmm = sem("hg_qkmm")
        hg_o = sem("hg_o")
        hg_osq = sem("hg_osq")
        hg_omm = sem("hg_omm")
        hg_orstd = sem("hg_orstd")
        s5_dt = sem("s5_dt")
        s5_th = sem("s5_th")
        s5_trig = sem("s5_trig")
        s5_tab = sem("s5_tab")
        s5_cx = sem("s5_cx")
        s5_scan = sem("s5_scan")
        s5_xr = sem("s5_xr")
        s5_b = sem("s5_b")
        s5_bt = sem("s5_bt")
        s5_bu = sem("s5_bu")
        s5_rot = sem("s5_rot")
        s5_x = sem("s5_x")
        s5_y = sem("s5_y")
        s5_pre = sem("s5_pre")
        s5_gelu = sem("s5_gelu")
        s5_glu = sem("s5_glu")
        s5_sig = sem("s5_sig")
        lr_sp = sem("lr_sp")
        lr_xc = sem("lr_xc")
        lr_coef = sem("lr_coef")
        lr_mm = sem("lr_mm")
        lr_gates = sem("lr_gates")
        lr_ln = sem("lr_ln")
        lr_sq = sem("lr_sq")
        lr_gelu = sem("lr_gelu")
        mg_sq = sem("mg_sq")
        mg_mm = sem("mg_mm")
        mg_rstd = sem("mg_rstd")
        mixed = sem("mixed")
        wo_mm = sem("wo_mm")
        h_ready = sem("h_ready")
        n2_rstd = sem("n2_rstd")
        x2_ready = sem("x2_ready")
        x2t_mm = sem("x2t_mm")
        x2t_kept = sem("x2t_kept")
        logit_mm = sem("logit_mm")
        r_exp = sem("r_exp")
        r_expd = sem("r_expd")
        rank_mm = sem("rank_mm")
        routed = sem("routed")
        p_ready = sem("p_ready")
        pw_ready = sem("pw_ready")
        pw_half = sem("pw_half")
        gate_done, up_done, down_done = unit_free[1], unit_free[3], unit_free[5]
        gath_mm = sem("gath_mm")
        xg_kept = sem("xg_kept")
        silu_k = sem("silu_k")
        h_k = sem("h_k")
        pwt_mm = sem("pwt_mm")
        ht_mm = sem("ht_mm")
        pwt_k = sem("pwt_k")
        ht_k = sem("ht_k")
        y_k = sem("y_k")
        y_mm = sem("y_mm")
        ysum = sem("ysum")
        fin_sum = sem("fin_sum")
        fin_rstd = sem("fin_rstd")
        fin = sem("fin")
        dn_load = sem("dn_load")
        dn_own = sem("dn_own")
        dn_pe = sem("dn_pe")
        dn_act = sem("dn_act")
        dn_sq = sem("dn_sq")
        dn_dve = sem("dn_dve")

        OUT_BANK = ((0, 1), (2, 5))
        MERGE_BANK = (6, 7, 1, 7)
        LEVEL_BANK = (2, 6)

        def win(n):
            return ring[:, n * 2048:(n + 1) * 2048].rearrange("p (c j) -> p c j", c=DC)

        wo = spread[:, :].rearrange("p (c n) -> p c n", c=DC)
        xT_t = xs[:, :].rearrange("p (c t) -> p c t", c=DC)
        hN = xs[:, :].rearrange("p (b d) -> p b d", b=TB)
        cosT = spread[:, 0:2048].rearrange("p (j t) -> p j t", j=S5_T)
        sinT = spread[:, 2048:4096].rearrange("p (j t) -> p j t", j=S5_T)
        s5t = [spread[:, 4096 + 512 * i:4096 + 512 * (i + 1)].rearrange("p (j t) -> p j t", j=2) for i in range(4)]
        s5x = [spread[:, 6144 + 512 * i:6144 + 512 * (i + 1)].rearrange("p (j t) -> p j t", j=2) for i in range(2)]
        ang, angk = (spread[:, 6144 + 512 * i:6144 + 512 * (i + 1)].rearrange("p (r j n) -> p r j n", r=2, j=S5_T) for i in range(2))
        glu_w = xs[:, 0:1024].rearrange("p (b n) -> p b n", b=NB)
        s5_act, s5_gate = (xs[:, 1024 + 512 * i:1536 + 512 * i].rearrange("p (b t) -> p b t", b=NB) for i in range(2))
        bnat = [spread[:, 7680 + 256 * i:7680 + 256 * (i + 1)] for i in range(2)]
        bt_s5 = spread[:, 7680:8192].rearrange("p (k b n) -> p k b n", k=2, b=NB)
        cx = spread[:, 7168:7680].rearrange("p (k j c) -> p k j c", k=2, j=S5_T)
        lru_x, lru_a, lru_i, lru_s = (t.rearrange("p b t -> p (b t)") for t in s5t)
        lru_x3, lru_a3, lru_i3, lru_s3 = s5t
        mixT = [kept["hg"], kept["su"], pads["wag"], kept["lg"]]

        def mix_ap(n, b):
            t = mixT[n]
            return t[:, b, 1:SEQ + 1] if n == 2 else t[:, b, :]

        def mix3(n):
            t = mixT[n]
            return t[:, :, 1:SEQ + 1] if n == 2 else t[:, :, :]

        x2 = w(0, 4).rearrange("p (b d) -> p b d", b=TB)
        x2T = w(4, 4).rearrange("p (c t) -> p c t", c=DC)
        n2w = w(8, 2)
        fw = w(10, 2)
        lg = work[:, 12, 0:72].rearrange("p (b n) -> p b n", b=TB)
        rt = work[:, 13, :]
        M = work[:, 14, 0:64].rearrange("p (b e) -> p b e", b=TB)
        C = work[:, 14, 64:128 + 4].rearrange("p (b e) -> p b e", b=TB)
        KEY = work[:, 14, 160:160 + 68].rearrange("p (b e) -> p b e", b=TB)
        CR = work[:, 14, 256:320].rearrange("p (b e) -> p b e", b=TB)
        M0 = work[:, 14, 320:384].rearrange("p (b e) -> p b e", b=TB)
        M1 = work[:, 14, 384:448].rearrange("p (b e) -> p b e", b=TB)
        flag_i = sb("flag_i", [1, 1], I32)
        xg = spread[:, 0:1024].rearrange("p (c s) -> p c s", c=DC)
        sg = spread[:, 1024:1536]
        hb = spread[:, 1536:2048]
        hT = spread[:, 2048:2560].rearrange("p (c s) -> p c s", c=FC)
        Yb = spread[:, 2560:3584]
        Pm = spread[:, 3584:3840].rearrange("p (b s) -> p b s", b=TB)
        PW = spread[:, 3840:4096].rearrange("p (b s) -> p b s", b=TB)
        PWT = spread[:, 4096:4352]
        junk = spread[:, 4352:5376]

        def unit_w(u, ab):
            return ring[:, u * UNIT + ab * 2048:u * UNIT + (ab + 1) * 2048]

        def extra_w(u, ab):
            if u == 0:
                return early[:, ab * 2048:(ab + 1) * 2048]
            return (spread[:, 5632:7680], w(4, 4))[ab]

        wg_d = w_gate.rearrange("e (p c) f -> e p (c f)", p=P)
        wu_d = w_up.rearrange("e (p c) f -> e p (c f)", p=P)
        wd_d = w_down.rearrange("e (p c) d -> e p (c d)", p=P)

        block = ctx.enter_context(nc.Block())

        @block.sync
        def _(sp):
            for k in range(2):
                sp.dma_start(xs[:, 1024 * k:1024 * (k + 1)], xT[:, 1024 * k:1024 * (k + 1)]).then_inc((s_x0, s_x)[k], 16)
            sp.dma_start(par[:, :], params).then_inc(s_x, 16)
            sp.dma_start(win(0), w_in[0]).then_inc(s_win[0], 16)
            sp.dma_start(sml[:, :], small).then_inc(s_small, 16)
            for n in range(1, 11):
                sp.dma_start(win(n), w_in[n]).then_inc(s_win[n], 16)

            def load_unit(u, e):
                for ab in range(2):
                    src = (wg_d, wg_d, wu_d, wu_d, wd_d, wd_d)[u]
                    sp.dma_start(unit_w(u, ab), src[e + ab, :, (u % 2) * 2048:(u % 2 + 1) * 2048]).then_inc(unit_full[u], 16)

            for u in range(UNITS):
                sp.wait_ge(proj_mm, min(2 * u + 2, 11))
                load_unit(u, 0)
            sp.dma_start(xs[:, 0:1024], glu).then_inc(s_xnat, 16)
            sp.wait_ge(s5_y, 4)
            sp.dma_start(wo, w_out.rearrange("(c p) n -> p c n", p=P)).then_inc(s_wout, 16)
            sp.wait_ge(mg_sq, 3)
            sp.dma_start(hN, x.rearrange("(b p) d -> p b d", p=P)).then_inc(s_xnat, 16)
            sp.wait_ge(mixed, 4)
            sp.dma_start(rout, router).then_inc(s_rows, 16)
            sp.dma_start(n2w, norm2_w.partition_broadcast(P)).then_inc(s_rows, 16)
            sp.dma_start(fw, final_w.partition_broadcast(P)).then_inc(s_rows, 16)
            sp.wait_ge(wo_mm, 4)
            for u in range(2):
                for ab in range(2):
                    if (u, ab) == (1, 1):
                        sp.wait_ge(logit_mm, 2)
                    sp.dma_start(extra_w(u, ab), wg_d[2 + ab, :, u * 2048:(u + 1) * 2048]).then_inc(extra_full[u], 16)
            for u in range(2):
                sp.wait_ge(unit_free[u], 1)
                load_unit(u, 4)
            for i in (1, 2):
                for u in range(2, UNITS):
                    sp.wait_ge(unit_free[u], i)
                    load_unit(u, 2 * i)
            with sp.Fori(3, PAIRS) as i:
                for u in range(UNITS):
                    sp.wait_ge(unit_free[u], i)
                    load_unit(u, 2 * i)
            sp.wait_ge(routed, 2)
            flag = sp.value_load(flag_i[0:1, 0:1], min_val=0, max_val=1)
            with sp.If(flag > 0):
                with sp.Fori(0, N_EXPERTS) as e:
                    sp.wait_ge(dn_pe, e * 6 + 1)
                    for k, src in enumerate((wg_d, wu_d, wd_d)):
                        sp.dma_start(ring[:, k * UNIT:(k + 1) * UNIT], src[e]).then_inc(dn_load, 16)
            with sp.Else():
                sp.nop()
            for b in range(TB):
                for n in range(2):
                    sp.wait_ge(fin, 2 * b + n + 1)
                    half = slice(n * 512, (n + 1) * 512)
                    sp.dma_start(out.rearrange("(b p) d -> b p d", p=P)[b, :, half], hN[:, b, half]).then_inc(s_out, 16)
            sp.wait_ge(s_out, 64)

        @block.gpsimd
        def _(pool):
            G = nc.gpsimd
            n = [0]

            def link(ins):
                n[0] += 1
                ins.then_inc(g_own, 1)
                pool.wait_ge(g_own, n[0])

            for t in ("wag", "k", "r", "v"):
                link(G.memset(pads[t][:, :, 0:1], 0.0))
            link(G.memset(lxp[:, :, 0:3], 0.0))
            link(G.memset(ones[:, :], 1.0))
            link(G.memset(headsum[:, :], 0.0))
            link(G.memset(headsum[0:64, 0:64], 1.0))
            link(G.memset(headsum[64:128, 64:128], 1.0))
            link(G.memset(cst[:, 0:1], RMS_EPS))
            link(G.memset(cst[:, 1:2], 10 * math.log(2.0)))
            link(G.memset(cst[:, 2:3], GN_EPS))
            link(G.memset(cst[:, 3:4], 1.0))
            G.memset(cst[:, 4:5], 0.0).then_inc(consts, 1)
            link(G.memset(ident[:, :], 0.0))
            G.affine_select(out=ident[:, :], in_=ident[:, :], compare_op=ALU.not_equal, fill=1.0, base=0,
                            pattern=[[-1, P]], channel_multiplier=1).then_inc(consts, 1)
            link(G.iota(xor_i[0:64, 0, :], pattern=[[0, CH]], base=0, channel_multiplier=1))
            link(G.iota(xor_i[64:128, 0, :], pattern=[[0, CH]], base=0, channel_multiplier=1))
            G.iota(xor_i[:, 1, :], pattern=[[1, CH]], base=0, channel_multiplier=0).then_inc(consts, 1)
            for r in range(2):
                link(G.iota(ang[:, r, :, 0:16], pattern=[[0, S5_T], [1, 16]], base=0, channel_multiplier=0,
                            allow_small_or_imprecise_dtypes=True))
                ins = G.iota(ang[:, r, :, 16:32], pattern=[[0, S5_T], [16, 16]], base=0, channel_multiplier=0,
                             allow_small_or_imprecise_dtypes=True)
                if r == 0:
                    link(ins)
            ins.then_inc(consts, 1)
            link(G.memset(bnat[0], 0.0))
            G.memset(bnat[1], 0.0).then_inc(consts, 1)
            pool.wait_ge(s5_trig, 1)
            sn, cs = ang[:, 0, :, :], ang[:, 1, :, :]

            def outer(hi, lo):
                return (hi[:, :, 16:32].unsqueeze(3).broadcast_to([P, S5_T, 16, 16]),
                        lo[:, :, 0:16].unsqueeze(2).broadcast_to([P, S5_T, 16, 16]))

            c4, s4 = (t.rearrange("p j (a b) -> p j a b", a=16) for t in (cosT, sinT))
            tmp = spread[:, 4096:6144].rearrange("p (j a b) -> p j a b", j=S5_T, a=16)
            link(G.tensor_tensor(c4, *outer(cs, cs), ALU.mult))
            link(G.tensor_tensor(tmp, *outer(sn, sn), ALU.mult))
            link(G.tensor_tensor(cosT, cosT, tmp.rearrange("p j a b -> p j (a b)"), ALU.subtract))
            link(G.tensor_tensor(s4, *outer(sn, cs), ALU.mult))
            link(G.tensor_tensor(tmp, *outer(cs, sn), ALU.mult))
            G.tensor_tensor(sinT, sinT, tmp.rearrange("p j a b -> p j (a b)"), ALU.add).then_inc(s5_tab, 1)
            pool.wait_ge(s5_tab, 1)
            lr, li = pcs("lr"), pcs("li")
            pool.wait_ge(s5_dt, 2)
            S = [s5c[:, k, :] for k in range(16)]
            link(G.tensor_tensor(S[4], S[1], cs[:, :, 1], ALU.mult))
            link(G.tensor_scalar(S[4], S[4], -1.0, None, ALU.add))
            link(G.tensor_tensor(S[5], S[1], sn[:, :, 1], ALU.mult))
            link(G.tensor_tensor(S[8], S[4], lr, ALU.mult))
            link(G.tensor_tensor(S[9], S[5], li, ALU.mult))
            link(G.tensor_tensor(S[8], S[8], S[9], ALU.add))
            link(G.tensor_tensor(S[8], S[8], S[7], ALU.mult))
            link(G.tensor_tensor(S[9], S[5], lr, ALU.mult))
            link(G.tensor_tensor(S[10], S[4], li, ALU.mult))
            link(G.tensor_tensor(S[9], S[9], S[10], ALU.subtract))
            link(G.tensor_tensor(S[9], S[9], S[7], ALU.mult))
            pool.wait_ge(s_small, 16)
            pool.wait_ge(consts, 5)

            def by_tile(name):
                return sc(name).rearrange("p (j c) -> p j c", j=S5_T)

            t1 = angk[:, 0, :, 0:16]
            t2 = angk[:, 1, :, 0:16]
            for k, (p1, p2, op) in enumerate((("bre", "bim", ALU.subtract), ("bim", "bre", ALU.add))):
                link(G.tensor_tensor(t1, by_tile(p1), S[8].unsqueeze(2).broadcast_to([P, S5_T, 16]), ALU.mult))
                link(G.tensor_tensor(t2, by_tile(p2), S[9].unsqueeze(2).broadcast_to([P, S5_T, 16]), ALU.mult))
                dst = bnat[k].rearrange("p (j c) -> p j c", j=S5_T)
                for h in range(2):
                    r = slice(64 * h, 64 * h + 64)
                    ins = G.tensor_tensor(dst[r, :, 16 * h:16 * h + 16], t1[r], t2[r], op)
                    if (k, h) == (1, 1):
                        ins.then_inc(s5_b, 1)
                        pool.wait_ge(s5_b, 1)
                    else:
                        link(ins)
            link(G.memset(cx, 0.0))
            for h in range(2):
                r = slice(64 * h, 64 * h + 64)
                link(G.tensor_copy(cx[r, 0, :, 16 * h:16 * h + 16], by_tile("cre")[r]))
                ins = G.tensor_scalar(cx[r, 1, :, 16 * h:16 * h + 16], by_tile("cim")[r], -1.0, None, ALU.mult)
                if h:
                    ins.then_inc(s5_cx, 1)
                    pool.wait_ge(s5_cx, 1)
                else:
                    link(ins)
            for q in range(4):
                C2, S2 = cosT[:, 2 * q:2 * q + 2, :], sinT[:, 2 * q:2 * q + 2, :]
                u = lxp[:, :, 3:SEQ + 3]
                pool.wait_ge(s5_scan, q + 1)
                if q:
                    pool.wait_ge(s5_y, q)
                link(G.tensor_tensor(s5x[1], s5t[2], S2, ALU.mult))
                link(G.tensor_tensor(u, s5t[3], C2, ALU.mult))
                G.tensor_tensor(s5x[1], s5x[1], u, ALU.add).then_inc(s5_x, 1)
                pool.wait_ge(s5_x, q + 1)
            pool.wait_ge(mixed, 4)
            link(G.memset(prefix, 1.0))
            link(G.affine_select(out=prefix, in_=prefix, compare_op=ALU.is_gt, fill=0.0, base=0,
                                 pattern=[[1, P]], channel_multiplier=-1))
            link(G.iota(iota, pattern=[[1, SLOTS]], base=0, channel_multiplier=0,
                        allow_small_or_imprecise_dtypes=True))
            G.iota(iota32, pattern=[[1, N_EXPERTS]], base=0, channel_multiplier=0,
                   allow_small_or_imprecise_dtypes=True).then_inc(consts, 1)

        @block.tensor
        def _(pe):
            mm = pe.matmul
            pe.wait_ge(consts, 1)
            pe.wait_ge(sq_dve, 1)
            i = mm(ps[2][:, 0:SEQ], ones[:, :], w(0)[:, 0:SEQ], start=True, stop=True)
            i.then_inc(ms_mm, 1)
            AR = w(0, 2).rearrange("p (m r t) -> p m r t", m=NM, r=2)
            def project(g, b):
                if b == 0:
                    pe.wait_ge(s_win[g], 16)
                    if g >= 2:
                        pe.wait_ge(proj_kept, g - 1)
                for c in range(DC):
                    if g == 0 and b == 0:
                        pe.wait_ge(xn_ready, c + 1)
                    i = mm(ps[g % 2][:, b * SEQ:(b + 1) * SEQ], win(g)[:, c, b * P:(b + 1) * P],
                           xT_t[:, c, :], start=c == 0, stop=c == DC - 1)
                if b == NB - 1:
                    i.then_inc(proj_mm, 1)

            def lru_gates():
                pe.wait_ge(lr_xc, 1)
                pe.wait_ge(s5_bt, 1)
                for k, name in enumerate(("lwa", "lwx")):
                    wt = sc(name)
                    for b in range(NB):
                        for h in range(2):
                            r = slice(64 * h, 64 * h + 64)
                            i = mm(ps[(2, 7)[k]][r, b * SEQ:(b + 1) * SEQ], wt[r, b * 64:(b + 1) * 64], lru_x3[r, b, :], start=True, stop=True)
                i.then_inc(lr_mm, 1)

            for g in range(8):
                project(g, 0)
                if g == 7:
                    lru_gates()
                project(g, 1)
                if g == 2:
                    pe.wait_ge(s_small, 16)
                    pe.wait_ge(wag_act, 2)
                    wa, g2 = sc("wa2"), sc("g2")
                    for b in range(NB):
                        mm(ps[2][:, b * SEQ:(b + 1) * SEQ], wa[0:64, b * P:(b + 1) * P], pads["wag"][0:64, 0, 1:SEQ + 1], start=True, stop=True)
                    for b in range(NB):
                        mm(ps[3][:, b * SEQ:(b + 1) * SEQ], wa[64:128, b * P:(b + 1) * P], pads["wag"][64:128, 0, 1:SEQ + 1], start=True, stop=True)
                    for b in range(NB):
                        i = mm(ps[4][:, b * SEQ:(b + 1) * SEQ], g2[:, b * P:(b + 1) * P], pads["wag"][:, 1, 1:SEQ + 1], start=True, stop=True)
                    i.then_inc(lora_mm, 1)
                    pe.wait_ge(kk_sq, 1)
                    mm(ps[5], headsum[:, :], w(8), start=True, stop=True).then_inc(head_mm, 1)
                if g == 4:
                    pe.wait_ge(rk_ready, 2)
                    mm(ps[6], headsum[:, :], w(4), start=True, stop=True).then_inc(head_mm, 1)
                if g == 5:
                    pe.wait_ge(s5_b, 1)
                    pe.wait_ge(consts, 2)
                    pe.wait_ge(lora_act, 5)
                    for k in range(2):
                        for b in range(NB):
                            i = pe.transpose(ps[2][:, (2 * k + b) * P:(2 * k + b + 1) * P], bnat[k][:, b * P:(b + 1) * P], ident[:, :])
                    i.then_inc(s5_bu, 1)
                if g == 6:
                    pe.wait_ge(scaled, 1)
                    pe.wait_ge(kk_max, 1)
                    pe.wait_ge(rk_ready, 3)
                    for k, src in enumerate((w(2), w(3))):
                        for m in range(NM):
                            for h in range(2):
                                r = slice(64 * h, 64 * h + 64)
                                i = mm(ps[3 + 2 * k + m // 4][r, (m % 4) * 128:(m % 4 + 1) * 128], src[r, m * CH:(m + 1) * CH],
                                       AR[r, m, :, :].rearrange("p r t -> p (r t)"), start=True, stop=True)
                        i.then_inc(score_mm, 1)
            def merge(n):
                pe.wait_ge(mg_sq, n + 1)
                if n >= 2:
                    pe.wait_ge(mg_rstd, n)
                for b in range(NB):
                    i = mm(ps[MERGE_BANK[n]][:, 0:SEQ], ones[:, :], w(17)[:, b * SEQ:(b + 1) * SEQ], start=b == 0, stop=b == NB - 1)
                i.then_inc(mg_mm, 1)

            def s5_inputs(q):
                if q:
                    pe.wait_ge(s5_rot, q)
                for jj in range(2):
                    for k in range(2):
                        j = 2 * q + jj
                        r = slice(32 * (j % 4), 32 * (j % 4) + 32)
                        i = mm(ps[(2, 7)[jj]][:, k * SEQ:(k + 1) * SEQ], bt_s5[r, k, j // 4, :],
                               kept["su"][r, j // 4, :], start=True, stop=True)
                i.then_inc(s5_bu, 1)

            def s5_outputs(q):
                pe.wait_ge(s5_cx, 1)
                pe.wait_ge(s5_xr, q + 1)
                pe.wait_ge(s5_x, q + 1)
                if q == 0:
                    pe.wait_ge(mg_rstd, 1)
                for jj in range(2):
                    j = 2 * q + jj
                    o = ps[6][32 * (j % 4):32 * (j % 4) + 32, (j // 4) * SEQ:(j // 4 + 1) * SEQ]
                    mm(o, cx[:, 0, j, :], s5x[0][:, jj, :], start=True, stop=False)
                    i = mm(o, cx[:, 1, j, :], s5x[1][:, jj, :], start=False, stop=True)
                i.then_inc(s5_y, 1)

            pe.wait_ge(vconst, 1)
            for k in range(3):
                pe.wait_ge(score_kept, k + 1)
                for m in range(NM):
                    for h in range(2):
                        r = slice(64 * h, 64 * h + 64)
                        b, c = m // NCH, m % NCH
                        src = pads["v"][r, b, 1 + c * CH:1 + (c + 1) * CH] if k == 0 else w(1 + k)[r, m * CH:(m + 1) * CH]
                        i = mm(ps[3 + k][r, m * CH:(m + 1) * CH], src, ident64[r, :], start=True, stop=True)
                i.then_inc(nat_mm, 1)
            def blocks(bank, lhs, rhs, done):
                for m in range(NM):
                    for h in range(2):
                        r = slice(64 * h, 64 * h + 64)
                        i = mm(ps[bank][r, m * CH:(m + 1) * CH], lhs[r, m * CH:(m + 1) * CH],
                               ident64[r, :] if rhs is None else rhs[r, m * CH:(m + 1) * CH], start=True, stop=True)
                i.then_inc(done, 1)

            pe.wait_ge(lev_m, 1)
            pe.wait_ge(nat_kept, 1)
            blocks(3, w(14), None, lev_p)
            for l in range(1, LEVELS):
                if l < 4:
                    project(7 + l, 0)
                pe.wait_ge(lev_m, l + 1)
                pe.wait_ge(lev_xk, 2 * l)
                blocks(3, w(14), w(11), lev_p)
                if l == 1:
                    pe.wait_ge(lr_gates, 4)
                    s5_inputs(0)
                if l == 2:
                    merge(0)
                if l >= 3:
                    s5_outputs(l - 3)
                if l < 4:
                    project(7 + l, 1)
                pe.wait_ge(lev_pk, l)
                pe.wait_ge(nat_kept, 3)
                if l < LEVELS - 1:
                    blocks(4, w(12), w(13), lev_x)
                blocks(5, w(13), w(12), lev_x)
                if 2 <= l < LEVELS - 1:
                    s5_inputs(l - 1)
            pe.wait_ge(lev_xk, 2 * LEVELS - 1)
            for c in range(NCH):
                if c >= 1:
                    pe.wait_ge(ch_sk, 2 * c)
                for b in range(NB):
                    m = b * NCH + c
                    for h in range(2):
                        r = slice(64 * h, 64 * h + 64)
                        o = ps[3][r, b * CH:(b + 1) * CH]
                        i = mm(o, w(8)[r, m * CH:(m + 1) * CH], w(4)[r, m * CH:(m + 1) * CH], start=True, stop=c == 0)
                        if c >= 1:
                            i = mm(o, AR[r, m, 0, :], state[r, c % 2, b, :], start=False, stop=True)
                i.then_inc(ch_rhs, 1)
                pe.wait_ge(ch_rhsk, c + 1)
                for b in range(NB):
                    m = b * NCH + c
                    for h in range(2):
                        r = slice(64 * h, 64 * h + 64)
                        i = mm(ps[4][r, b * CH:(b + 1) * CH], w(12)[r, m * CH:(m + 1) * CH], rhs_t[r, b, :], start=True, stop=True)
                i.then_inc(ch_u, 1)
                pe.wait_ge(ch_uk, c + 1)
                if c < NCH - 1:
                    for b in range(NB):
                        m = b * NCH + c
                        for h in range(2):
                            r = slice(64 * h, 64 * h + 64)
                            o = ps[5][r, b * CH:(b + 1) * CH]
                            mm(o, w(5)[r, m * CH:(m + 1) * CH], u_t[r, b, :], start=True, stop=False)
                            i = mm(o, w(6)[r, m * CH:(m + 1) * CH], w(4)[r, m * CH:(m + 1) * CH], start=False, stop=True)
                    i.then_inc(ch_s, 1)
                for b in range(NB):
                    m = b * NCH + c
                    for h in range(2):
                        r = slice(64 * h, 64 * h + 64)
                        o = ps[0][r, m * CH:(m + 1) * CH]
                        mm(o, u_t[r, b, :], w(9)[r, m * CH:(m + 1) * CH], start=True, stop=False)
                        i = mm(o, w(4)[r, m * CH:(m + 1) * CH], w(10)[r, m * CH:(m + 1) * CH], start=False, stop=c == 0)
                        if c >= 1:
                            i = mm(o, state[r, c % 2, b, :], AR[r, m, 1, :], start=False, stop=True)
                i.then_inc(ch_y, 1)
                if c == 0:
                    s5_outputs(3)

            def s5_glu_half(k):
                for ob in (2 * k, 2 * k + 1):
                    for b in range(NB):
                        i = mm(ps[1 + k][:, (ob % 2) * SEQ:(ob % 2 + 1) * SEQ], glu_w[:, b, ob * P:(ob + 1) * P],
                               s5_act[:, b, :], start=b == 0, stop=b == NB - 1)
                i.then_inc(s5_glu, 1)

            pe.wait_ge(s5_gelu, 1)
            pe.wait_ge(s_xnat, 16)
            s5_glu_half(0)
            pe.wait_ge(y_kept, 1)
            mm(ps[6], headsum[:, :], w(17), start=True, stop=True).then_inc(gn_mm, 1)
            s5_glu_half(1)
            pe.wait_ge(gn_sq, 1)
            mm(ps[7], headsum[:, :], w(13), start=True, stop=True).then_inc(gn_mm, 1)

            def project_out(mixers, tb, n, first=False, last=False):
                for q in mixers:
                    for b in range(NB):
                        i = mm(ps[OUT_BANK[tb][n]], mix_ap(q, b)[:, tb * P:(tb + 1) * P], wo[:, 2 * q + b, n * 512:(n + 1) * 512],
                               start=first and q == mixers[0] and b == 0, stop=last and b == NB - 1)
                if last:
                    i.then_inc(wo_mm, 1)

            pe.wait_ge(hg_gates, 2)
            for b in range(NB):
                for tb in range(TB):
                    i = pe.transpose(ps[3][:, tb * 256 + b * P:tb * 256 + (b + 1) * P], kept["hi"][:, b, tb * P:(tb + 1) * P], ident[:, :])
            i.then_inc(hg_vt, 1)
            for li, L in enumerate(HG_LEVELS):
                pe.wait_ge(hg_scaled, li + 1)
                if li == 2:
                    pe.wait_ge(hg_vn, 1)
                    pe.wait_ge(s5_sig, 1)
                if li == 3:
                    pe.wait_ge(mg_rstd, 2)
                if li >= 4:
                    pe.wait_ge(hg_sck, li - 3)
                for hd in range(4):
                    e, b = hd % 2, hd // 2
                    r = slice(64 * e, 64 * e + 64)
                    t = w3(li)[r, b, :]
                    if L == 128:
                        i = mm(ps[4 + e][:, b * P:(b + 1) * P], t[:, 0:P], t[:, P:SEQ], start=True, stop=True)
                        continue
                    for hf in range(2):
                        if L == 64:
                            i = mm(ps[4 + e][0:64, 256 + (b * 2 + hf) * 64:256 + (b * 2 + hf + 1) * 64], t[:, hf * P:hf * P + 64],
                                   t[:, hf * P + 64:hf * P + 128], start=True, stop=True)
                            continue
                        for q in range(2):
                            ts_ = slice(hf * P + 64 * q, hf * P + 64 * q + 64)
                            i = mm(ps[LEVEL_BANK[li % 2] + e][64 * q:64 * q + 64, (b * 2 + hf) * 64:(b * 2 + hf + 1) * 64], t[:, ts_], t[:, ts_],
                                   start=True, stop=True)
                i.then_inc(hg_sc, 1)
                if li == 1:
                    pe.wait_ge(gn_rstd, 1)
                    merge(1)
                if li == 2:
                    pe.wait_ge(s_wout, 16)
                    project_out((3,), 0, 0, first=True)
                if li == 3:
                    pe.wait_ge(mixed, 2)
                    project_out((2,), 0, 0)
                if li == 4:
                    merge(2)
                if li == 6:
                    pe.wait_ge(mg_rstd, 3)
                    project_out((3, 2), 0, 1, first=True)
            pe.wait_ge(hg_qk, 1)
            pe.wait_ge(hg_sck, 5)
            mm(ps[3], headsum[:, :], flat(kept["hf"]), start=True, stop=True).then_inc(hg_qkmm, 1)
            pe.wait_ge(hg_sck, 7)
            vn = w(10).rearrange("p (t c) -> p t c", t=TB)
            SC = w(15, 2).rearrange("p (e b f t) -> p b e f t", e=2, b=NB, f=2)
            SX = w(13).rearrange("p (e b t) -> p b e t", e=2, b=NB)
            for hd in range(4):
                r = slice(64 * (hd % 2), 64 * (hd % 2) + 64)
                b = hd // 2
                cs = slice(hd * 64, hd * 64 + 64)
                mm(ps[6][r, b * SEQ:b * SEQ + P], vn[:, 0, cs], SC[:, b, hd % 2, 0, :], start=True, stop=True)
                mm(ps[6][r, b * SEQ + P:(b + 1) * SEQ], vn[:, 1, cs], SC[:, b, hd % 2, 1, :], start=True, stop=False)
                i = mm(ps[6][r, b * SEQ + P:(b + 1) * SEQ], vn[:, 0, cs], SX[:, b, hd % 2, :], start=False, stop=True)
            i.then_inc(hg_o, 1)
            pe.wait_ge(mixed, 3)
            project_out((1,), 0, 0)
            pe.wait_ge(hg_osq, 1)
            mm(ps[4], headsum[:, :], w(0), start=True, stop=True).then_inc(hg_omm, 1)
            project_out((1,), 0, 1)
            project_out((1, 2, 3), 1, 0, first=True)
            merge(3)
            project_out((1, 2), 1, 1, first=True)
            pe.wait_ge(mixed, 4)
            for n in range(2):
                project_out((0,), 0, n, last=True)
            project_out((3,), 1, 1)
            for n in range(2):
                project_out((0,), 1, n, last=True)
            for tb in range(TB):
                pe.wait_ge(x2_ready, tb + 1)
                for c in range(DC):
                    i = pe.transpose(ps[2 * tb + c // 4][:, (c % 4) * P:(c % 4 + 1) * P], x2[:, tb, c * P:(c + 1) * P], ident[:, :])
                i.then_inc(x2t_mm, 1)
            pe.wait_ge(s_rows, 48)
            router = rout[:, 0:DC * 36].rearrange("p (c n) -> p c n", c=DC)
            for tb in range(TB):
                pe.wait_ge(x2t_kept, 2 * tb + 2)
                for c in range(DC):
                    i = mm(ps[6 + tb][:, 0:36], x2T[:, c, tb * P:(tb + 1) * P], router[:, c, :], start=c == 0, stop=c == DC - 1)
                i.then_inc(logit_mm, 1)
            pe.wait_ge(x2t_kept, 4)
            pe.wait_ge(y_k, 2)
            pe.wait_ge(pwt_k, 1)
            for k in range(4):
                mm(ps[k], PWT[:, 0:P], Yb[:, 0:512], start=True, stop=False, skip_group_check=True)
            pe.wait_ge(r_exp, 2)
            pe.wait_ge(consts, 6)
            mm(ps[4][:, 0:32], prefix, M[:, 0, :], start=True, stop=True)
            mm(ps[4][:, 32:64], prefix, M[:, 1, :], start=True, stop=False)
            mm(ps[4][:, 32:64], ones[:, :], M[:, 0, :], start=False, stop=True)
            mm(ps[4][:, 64:96], ones[:, :], M[:, 0, :], start=True, stop=False)
            mm(ps[4][:, 64:96], ones[:, :], M[:, 1, :], start=False, stop=True).then_inc(rank_mm, 1)

            gB, uB, d0, d1 = ps[4], ps[5], ps[6], ps[7]
            pe.wait_ge(routed, 2)

            def gather():
                for c in range(DC):
                    for tb in range(TB):
                        i = mm((d0, d1)[c // 4][:, (c % 4) * P:(c % 4 + 1) * P], x2[:, tb, c:D_MODEL:DC], Pm[:, tb, :],
                               start=tb == 0, stop=tb == TB - 1)
                i.then_inc(gath_mm, 1)

            def scatter(last=False):
                for tb in range(TB):
                    for n in range(2):
                        i = mm(ps[2 * tb + n], PWT[:, tb * P:(tb + 1) * P], Yb[:, n * 512:(n + 1) * 512],
                               start=False, stop=False, skip_group_check=True)
                    if last:
                        i.then_inc(y_mm, 1)

            pe.wait_ge(p_ready, 1)
            gather()
            def pair(i, which=None):
                def products(bank, u0):
                    for u in (u0, u0 + 1):
                        extra = u < 2 and which == 1
                        if extra:
                            pe.wait_ge(extra_full[u], 32)
                        elif u < 2 and which != 0:
                            pe.wait_ge(unit_full[u], i * 32)
                        else:
                            pe.wait_ge(unit_full[u], i * 32 + 32)
                        for cc in range(4):
                            c = (u - u0) * 4 + cc
                            for ab in range(2):
                                m_ = mm(bank[64 * ab:64 * ab + 64, :], xg[:, c, 64 * ab:64 * ab + 64],
                                        (extra_w(u, ab) if extra else unit_w(u, ab))[:, cc * 512:(cc + 1) * 512],
                                        start=c == 0, stop=c == DC - 1)
                        m_.then_inc(unit_free[u], 1)

                pe.wait_ge(xg_kept, i * 2 + 2)
                pe.wait_ge(ht_k, i + 1)
                products(gB, 0)
                if which != 0:
                    pe.wait_ge(y_k, i * 2 + 2)
                    pe.wait_ge(pwt_k, i + 1)
                    scatter()
                products(uB, 2)
                if which != PAIRS - 1:
                    pe.wait_ge(p_ready, i + 2)
                    gather()
                pe.wait_ge(h_k, i + 1)
                for c in range(FC):
                    m_ = pe.transpose(gB[:, c * P:(c + 1) * P], hb[:, c:D_EXPERT:FC], ident[:, :])
                m_.then_inc(ht_mm, 1)
                pe.wait_ge(pw_ready, i + 1)
                for tb in range(TB):
                    m_ = pe.transpose(uB[:, tb * P:(tb + 1) * P], PW[:, tb, :], ident[:, :])
                m_.then_inc(pwt_mm, 1)
                pe.wait_ge(ht_k, i + 2)
                if which != PAIRS - 1:
                    pe.wait_ge(xg_kept, i * 2 + 4)
                for u in (4, 5):
                    pe.wait_ge(unit_full[u], i * 32 + 32)
                    for cc in range(2):
                        c = (u - 4) * 2 + cc
                        for n in range(2):
                            for ab in range(2):
                                m_ = mm((d0, d1)[n][64 * ab:64 * ab + 64, :], hT[:, c, 64 * ab:64 * ab + 64],
                                        unit_w(u, ab)[:, cc * 1024 + n * 512:cc * 1024 + (n + 1) * 512], start=c == 0, stop=c == FC - 1)
                    m_.then_inc(unit_free[u], 1)

            pair(0, 0)
            pair(1, 1)
            with pe.Fori(2, PAIRS - 1) as i:
                pair(i)
            pair(PAIRS - 1, PAIRS - 1)
            pe.wait_ge(y_k, 2 * PAIRS + 2)
            pe.wait_ge(pwt_k, PAIRS + 1)
            scatter(last=True)

            flag = pe.value_load(flag_i[0:1, 0:1], min_val=0, max_val=1)
            with pe.If(flag > 0):
                pe.wait_ge(ysum, 2)
                for tb in range(TB):
                    for c in range(DC):
                        i = pe.transpose(ps[2 * tb + c // 4][:, (c % 4) * P:(c % 4 + 1) * P], x2[:, tb, c:D_MODEL:DC], ident[:, :])
                i.then_inc(dn_pe, 1)
                pe.wait_ge(dn_dve, 1)
                with pe.Fori(0, N_EXPERTS) as e:
                    pe.wait_ge(dn_load, e * 48 + 48)
                    wgs = ring[:, 0:UNIT].rearrange("p (c f) -> p c f", c=DC)
                    wus = ring[:, UNIT:2 * UNIT].rearrange("p (c f) -> p c f", c=DC)
                    wds = ring[:, 2 * UNIT:3 * UNIT].rearrange("p (c d) -> p c d", c=FC)
                    for tb in range(TB):
                        for c in range(DC):
                            mm(gB[:, :], x2T[:, c, tb * P:(tb + 1) * P], wgs[:, c, :], start=c == 0, stop=c == DC - 1)
                        for c in range(DC):
                            m_ = mm(uB[:, :], x2T[:, c, tb * P:(tb + 1) * P], wus[:, c, :], start=c == 0, stop=c == DC - 1)
                        m_.then_inc(dn_pe, 1)
                        pe.wait_ge(dn_dve, e * 6 + 3 * tb + 2)
                        for c in range(FC):
                            m_ = pe.transpose(gB[:, c * P:(c + 1) * P], hb[:, c:D_EXPERT:FC], ident[:, :])
                        m_.then_inc(dn_pe, 1)
                        pe.wait_ge(dn_dve, e * 6 + 3 * tb + 3)
                        for n in range(2):
                            for c in range(FC):
                                m_ = mm((d0, d1)[n][:, :], hT[:, c, :], wds[:, c, n * 512:(n + 1) * 512], start=c == 0, stop=c == FC - 1)
                        m_.then_inc(dn_pe, 1)
                        pe.wait_ge(dn_dve, e * 6 + 3 * tb + 4)
            with pe.Else():
                pe.nop()

        @block.scalar
        def _(act):
            A = nc.scalar
            n_own = [0]

            def link(ins):
                n_own[0] += 1
                ins.then_inc(a_own, 1)
                act.wait_ge(a_own, n_own[0])

            act.wait_ge(consts, 1)
            act.wait_ge(s_x0, 16)
            A.activation(w(0, 2), xs[:, 0:1024], ACT.Square).then_inc(sq_act, 1)
            act.wait_ge(s_x, 32)

            def inv_sqrt(src, dst, eps_col, scale, ready):
                link(A.activation(dst, src, ACT.Ln, bias=cst[:, eps_col:eps_col + 1], scale=scale))
                A.activation(dst, dst, ACT.Exp, scale=-0.5).then_inc(ready, 1)

            act.wait_ge(ms_mm, 1)
            inv_sqrt(ps[2][:, 0:SEQ], rstd[:, :], 0, 1.0 / D_MODEL, rstd1)

            def keep(g):
                name = GROUPS[g]
                act.wait_ge(proj_mm, g + 1)
                src = ps[g % 2].rearrange("p (b t) -> p b t", b=NB)
                t = kept[name]
                off = {"wag": 1, "k": 1, "r": 1, "v": 1, "lx": 3}.get(name, 0)
                A.copy(t[:, :, off:off + SEQ], src).then_inc(proj_kept, 1)

            link(A.activation(col[:, 0:2], pcs("lam"), ACT.Exp, scale=-1.0))
            A.activation(s5c[:, 0, :], pcs("ldt"), ACT.Exp).then_inc(s5_dt, 1)
            act.wait_ge(s5_th, 1)
            A.activation(s5c[:, 1, :], s5c[:, 1, :], ACT.Exp).then_inc(s5_dt, 1)
            A.activation(col[:, 0:2], col[:, 0:2], ACT.Ln, bias=cst[:, 3:4]).then_inc(lr_sp, 1)
            keep(0)
            act.wait_ge(s5_th, 2)
            A.activation(ang, ang, ACT.Sin).then_inc(s5_trig, 1)
            keep(1)
            act.wait_ge(wag_mixed, 1)
            A.activation(pads["wag"][0:64, 0, 1:SEQ + 1], pads["wag"][0:64, 0, 1:SEQ + 1], ACT.Tanh).then_inc(wag_act, 1)
            A.activation(pads["wag"][:, 1, 1:SEQ + 1], pads["wag"][:, 1, 1:SEQ + 1], ACT.Sigmoid).then_inc(wag_act, 1)
            keep(2)
            act.wait_ge(lora_mm, 1)
            for b in range(NB):
                A.activation(w3(9)[:, b, :], ps[2][:, b * SEQ:(b + 1) * SEQ], ACT.Sigmoid, bias=pc("w0", b)).then_inc(lora_act, 1)
            for b in range(NB):
                A.activation(w3(10)[:, b, :], ps[3][:, b * SEQ:(b + 1) * SEQ], ACT.Sigmoid, bias=pc("a0", b)).then_inc(lora_act, 1)
            A.copy(w(15), ps[4]).then_inc(lora_act, 1)
            keep(3)
            keep(4)
            act.wait_ge(rw_cum, 1)
            A.activation(w(12), w(11), ACT.Exp, scale=-RW_C).then_inc(rw_exp, 1)
            A.activation(w(13), w(11), ACT.Exp, scale=RW_C).then_inc(rw_exp, 1)
            act.wait_ge(rw_cum, 2)
            A.activation(w(14), w(9), ACT.Exp, scale=-RW_C).then_inc(rw_exp, 1)
            act.wait_ge(kk_max, 1)
            link(A.activation(w(8), w(8), ACT.Ln, scale=2.0 ** 20))
            A.activation(w(8), w(8), ACT.Exp, scale=-0.5, bias=cst[:, 1:2]).then_inc(kk_inv, 1)
            keep(5)
            act.wait_ge(s5_bu, 1)
            A.copy(bt_s5.rearrange("p a b c -> p (a b c)"), ps[2]).then_inc(s5_bt, 1)
            keep(6)
            act.wait_ge(lr_mm, 1)
            for b in range(NB):
                A.activation(lru_a3[:, b, :], ps[2][:, b * SEQ:(b + 1) * SEQ], ACT.Sigmoid, bias=pc("ba", b)).then_inc(lr_gates, 1)
            for b in range(NB):
                A.activation(lru_i3[:, b, :], ps[7][:, b * SEQ:(b + 1) * SEQ], ACT.Sigmoid, bias=pc("bx", b)).then_inc(lr_gates, 1)
            act.wait_ge(lr_coef, 1)
            act.wait_ge(lr_gates, 4)
            for b in range(NB):
                A.activation(lru_s3[:, b, :], lru_a3[:, b, :], ACT.Tanh, scale=col[:, 2 + b:3 + b]).then_inc(lr_gates, 1)
            keep(7)
            for k in range(3):
                act.wait_ge(nat_mm, k + 1)
                A.copy(w(4 + k), ps[3 + k]).then_inc(nat_kept, 1)
            for b in range(NB):
                A.activation(lru_a3[:, b, :], lru_a3[:, b, :], ACT.Exp, scale=col[:, 4 + b:5 + b]).then_inc(lr_gates, 1)
            act.wait_ge(lr_ln, 1)
            link(A.activation(lru_s, lru_s, ACT.Ln))
            A.activation(lru_s, lru_s, ACT.Exp, scale=0.5).then_inc(lr_sq, 1)
            A.activation(kept["lg"][:, :, :], kept["lg"][:, :, :], ACT.Gelu_apprx_tanh).then_inc(lr_gelu, 1)

            def merge(n):
                act.wait_ge(mg_mm, n + 1)
                if n:
                    act.wait_ge(mixed, n)
                link(A.activation(rstd[:, :], ps[MERGE_BANK[n]][:, 0:SEQ], ACT.Ln, bias=cst[:, 0:1], scale=1.0 / GROUP_W))
                A.activation(rstd[:, :], rstd[:, :], ACT.Exp, scale=-0.5).then_inc(mg_rstd, 1)

            def keep_p(l):
                act.wait_ge(lev_p, l + 1)
                A.copy(w(13), ps[3]).then_inc(lev_pk, 1)

            keep_p(1)
            keep(8)
            keep_p(2)
            keep(9)
            merge(0)
            keep_p(3)
            keep(10)
            keep_p(4)
            keep_p(5)
            act.wait_ge(s5_pre, 1)
            A.activation(s5_act, s5_act, ACT.Gelu_apprx_tanh).then_inc(s5_gelu, 1)
            for name in ("hq", "hi", "hg"):
                A.activation(flat(kept[name]), flat(kept[name]), ACT.Silu).then_inc(hg_gates, 1)
            A.activation(w(2), flat(kept["hf"]), ACT.Sigmoid).then_inc(hg_gates, 1)
            A.activation(flat(kept["hf"]), flat(kept["hf"]), ACT.Sigmoid, scale=-1.0).then_inc(hg_gates, 1)
            act.wait_ge(hg_f, 1)
            A.activation(w(2), w(2), ACT.Ln).then_inc(hg_ln, 1)
            act.wait_ge(ch_y, NCH)
            A.copy(w(17), ps[0]).then_inc(y_kept, 1)

            def level_exp(k):
                act.wait_ge(hg_diff, k + 1)
                d = w((8, 12)[k % 2]).rearrange("p (n two l) -> p n two l", two=2, l=HG_LEVELS[k])
                A.activation(d[:, :, 0, :], d[:, :, 0, :], ACT.Exp, scale=-1.0).then_inc(hg_e, 1)
                A.activation(d[:, :, 1, :], d[:, :, 1, :], ACT.Exp).then_inc(hg_e, 1)

            level_exp(0)
            level_exp(1)
            act.wait_ge(gn_mm, 2)
            link(A.activation(w(14), ps[7], ACT.Ln, bias=cst[:, 2:3], scale=1.0 / HEAD))
            A.activation(w(14), w(14), ACT.Exp, scale=-0.5).then_inc(gn_rstd, 1)
            act.wait_ge(hg_vt, 1)
            A.copy(w(10), ps[3]).then_inc(hg_vn, 1)
            level_exp(2)
            level_exp(3)
            act.wait_ge(s5_glu, 2)
            A.activation(s5_gate, ps[2].rearrange("p (b t) -> p b t", b=NB), ACT.Sigmoid).then_inc(s5_sig, 1)
            merge(1)
            level_exp(4)
            level_exp(5)
            level_exp(6)
            merge(2)
            level_exp(7)
            act.wait_ge(hg_omm, 1)
            link(A.activation(w(0), ps[4], ACT.Ln, bias=cst[:, 0:1], scale=1.0 / HEAD))
            A.activation(w(0), w(0), ACT.Exp, scale=-0.5).then_inc(hg_orstd, 1)
            merge(3)
            for tb in range(TB):
                act.wait_ge(h_ready, 2 * tb + 2)
                link(A.activation(w(14 + 2 * tb, 2), hN[:, tb, :], ACT.Square, accum_out=col[:, 8 + tb:9 + tb]))
                r = col[:, 10 + tb:11 + tb]
                link(A.activation(r, col[:, 8 + tb:9 + tb], ACT.Ln, bias=cst[:, 0:1], scale=1.0 / D_MODEL))
                A.activation(r, r, ACT.Exp, scale=-0.5).then_inc(n2_rstd, 1)
            for tb in range(TB):
                act.wait_ge(x2t_mm, tb + 1)
                for q in range(2):
                    A.copy(x2T[:, 4 * q:4 * q + 4, tb * P:(tb + 1) * P], ps[2 * tb + q].rearrange("p (c t) -> p c t", c=4)).then_inc(x2t_kept, 1)
            act.wait_ge(r_exp, 1)
            A.activation(work[:, 12, 80:96].rearrange("p (b n) -> p b n", b=TB), work[:, 12, 96:112].rearrange("p (b n) -> p b n", b=TB), ACT.Exp).then_inc(r_expd, 1)
            act.wait_ge(gath_mm, 1)

            def keep_xg():
                for q in range(2):
                    A.copy(xg[:, 4 * q:4 * q + 4, :].rearrange("p c s -> p (c s)"), ps[6 + q]).then_inc(xg_kept, 1)

            keep_xg()

            def pair(i, last=False):
                act.wait_ge(gate_done, i + 1)
                A.activation(sg, ps[4], ACT.Silu).then_inc(silu_k, 1)
                if not last:
                    act.wait_ge(gath_mm, i + 2)
                    keep_xg()
                act.wait_ge(down_done, i + 1)
                A.copy(Yb[:, 0:512], ps[6]).then_inc(y_k, 1)
                A.copy(Yb[:, 512:1024], ps[7]).then_inc(y_k, 1)

            with act.Fori(0, PAIRS - 1) as i:
                pair(i)
            pair(PAIRS - 1, last=True)
            def h_squares():
                for tb in range(TB):
                    act.wait_ge(ysum, tb + 1)
                    link(A.activation(junk, hN[:, tb, :], ACT.Square, accum_out=col[:, 12 + tb:13 + tb]))

            h_squares()
            flag = act.value_load(flag_i[0:1, 0:1], min_val=0, max_val=1)
            with act.If(flag > 0):
                with act.Fori(0, N_EXPERTS) as e:
                    for tb in range(TB):
                        act.wait_ge(dn_pe, e * 6 + 3 * tb + 2)
                        A.activation(sg, ps[4], ACT.Silu).then_inc(dn_act, 1)
                act.wait_ge(fin_sum, 1)
                for tb in range(TB):
                    A.activation(junk, hN[:, tb, :], ACT.Square, accum_out=col[:, 12 + tb:13 + tb]).then_inc(dn_sq, 1)
                    act.wait_ge(dn_sq, tb + 1)
            with act.Else():
                act.nop()
            link(A.activation(col[:, 14:16], col[:, 12:14], ACT.Ln, bias=cst[:, 0:1], scale=1.0 / D_MODEL))
            A.activation(col[:, 14:16], col[:, 14:16], ACT.Exp, scale=-0.5).then_inc(fin_rstd, 1)

        @block.vector
        def _(dve):
            V = nc.vector
            tt, ts, stt = V.tensor_tensor, V.tensor_scalar, V.scalar_tensor_tensor
            MUL, ADD, SUB = ALU.mult, ALU.add, ALU.subtract
            count = {}

            def link(ins, s=v_own):
                count[id(s)] = count.get(id(s), 0) + 1
                ins.then_inc(s, 1)
                dve.wait_ge(s, count[id(s)])

            dve.wait_ge(s_x, 32)
            link(tt(w(2, 2), xs[:, 1024:2048], xs[:, 1024:2048], MUL))
            dve.wait_ge(sq_act, 1)
            link(tt(w(0, 2), w(0, 2), w(2, 2), ADD))
            link(tt(w(0), w(0), w(1), ADD))
            link(tt(w(0)[:, 0:SEQ], w(0)[:, 0:SEQ], w(0)[:, SEQ:2 * SEQ], ADD), sq_dve)
            dve.wait_ge(rstd1, 1)
            for c in range(DC):
                link(stt(xT_t[:, c, :], xT_t[:, c, :], pc("norm1", c), rstd[:, :], MUL, MUL), xn_ready)

            dve.wait_ge(s5_dt, 1)
            lr, li = pcs("lr"), pcs("li")
            link(tt(s5c[:, 1, :], lr, s5c[:, 0, :], MUL), s5_th)
            th, kf = s5c[:, 2, :], s5c[:, 3, :]
            link(tt(th, li, s5c[:, 0, :], MUL))

            def reduce_angle(a, k):
                link(ts(k, a, 1.0 / TWO_PI, MAGIC, MUL, ADD))
                link(ts(k, k, -MAGIC, None, ADD))
                for part in (TP1, TP2, TP3):
                    link(stt(a, k, -part, a, MUL, ADD))

            reduce_angle(th, kf)
            dve.wait_ge(consts, 4)
            for r in range(2):
                link(tt(ang[:, r, :, :], ang[:, r, :, :], th.unsqueeze(2).broadcast_to([P, S5_T, 32]), MUL))
            link(ts(ang[:, 1, :, :], ang[:, 1, :, :], math.pi / 2, None, ADD))
            af = ang.rearrange("p r j n -> p (r j n)")
            reduce_angle(af, angk.rearrange("p r j n -> p (r j n)"))
            link(tt(s5c[:, 6, :], lr, lr, MUL))
            link(tt(s5c[:, 7, :], li, li, MUL))
            link(tt(s5c[:, 6, :], s5c[:, 6, :], s5c[:, 7, :], ADD))
            link(V.reciprocal(s5c[:, 7, :], s5c[:, 6, :]))
            link(ts(af, af, 3.141592, -3.141592, ALU.min, ALU.max), s5_th)
            def shift_mix(name, mu):
                t = pads[name]
                link(tt(w3(17), t[:, :, 0:SEQ], t[:, :, 1:SEQ + 1], SUB))
                for b in range(NB):
                    ins = stt(t[:, b, 1:SEQ + 1], w3(17)[:, b, :], pc("mu", mu + b), t[:, b, 1:SEQ + 1], MUL, ADD)
                    link(ins, wag_mixed if name == "wag" and b == 1 else v_own)

            def cumulate(dst, src, length, s=v_own):
                n = src.shape[1] // length
                for k in range(n):
                    t = slice(k * length, (k + 1) * length)
                    link(V.tensor_tensor_scan(dst[:, t], cst[:, 3:4].broadcast_to([P, length]), src[:, t], 0.0, MUL, ADD),
                         s if k == n - 1 else v_own)

            dve.wait_ge(proj_kept, 1)
            shift_mix("wag", 6)
            dve.wait_ge(consts, 3)
            link(V.tensor_copy(lev[:, 0:2, :], xor_i))
            link(tt(m_strict[:, :], lev[:, 0, :], lev[:, 1, :], ALU.is_lt))
            link(tt(m_incl[:, :], lev[:, 0, :], lev[:, 1, :], ALU.is_le))
            link(tt(xor_i[:, 0, :], xor_i[:, 0, :], xor_i[:, 1, :], ALU.bitwise_xor))
            link(V.tensor_copy(xor_f, xor_i[:, 0, :]))
            link(ts(ident64[:, :], xor_f, 0.0, None, ALU.is_equal))
            for l in range(LEVELS):
                link(ts(state[:, 0, 0, :], xor_f, float(2 ** (l + 1)), None, ALU.is_lt))
                link(stt(lev[:, l, :], xor_f, float(2 ** l), state[:, 0, 0, :], ALU.is_ge, MUL))
            link(tt(lev[:, :, :], lev[:, :, :], m_strict[:, :].unsqueeze(1).broadcast_to([P, LEVELS, CH]), MUL), vconst)

            k3, r3, v3 = (pads[n][:, :, 1:SEQ + 1] for n in ("k", "r", "v"))
            dve.wait_ge(proj_kept, 2)
            shift_mix("k", 2)
            for b in range(NB):
                link(ts(w3(7)[:, b, :], k3[:, b, :], pc("k_k", b), None, MUL))
            link(tt(w(8), w(7), w(7), MUL), kk_sq)
            dve.wait_ge(proj_kept, 3)
            shift_mix("r", 0)
            dve.wait_ge(lora_act, 2)
            cumulate(w(11), w(9), CH, rw_cum)
            link(tt(w(9), w(11), w(9), SUB), rw_cum)
            dve.wait_ge(lora_act, 4)
            for b in range(NB):
                link(ts(w3(5)[:, b, :], w3(10)[:, b, :], -1.0, pc("k_a", b), ADD, MUL))
            link(stt(w3(5), w3(5), 1.0, k3, ADD, MUL))
            for b in range(NB):
                link(stt(w3(4)[:, b, :], r3[:, b, :], pc("r_k", b), w3(5)[:, b, :], MUL, MUL), rk_ready)
            dve.wait_ge(head_mm, 1)
            link(ts(w(8), ps[5], 1e-24, None, ALU.max), kk_max)
            dve.wait_ge(proj_kept, 4)
            shift_mix("v", 4)
            dve.wait_ge(kk_inv, 1)
            link(tt(w(7), w(7), w(8), MUL))
            link(tt(w(6), w(7), w(10), MUL))
            AR = w(0, 2).rearrange("p (m r t) -> p m r t", m=NM, r=2)

            def by_chunk(t):
                return t.rearrange("p (m t) -> p m t", m=NM)

            dve.wait_ge(rw_exp, 3)
            link(stt(AR[:, :, 0, :], by_chunk(w(7)), -1.0, by_chunk(w(14)), MUL, MUL))
            for b in range(NB):
                link(tt(AR[:, b * NCH:(b + 1) * NCH, 1, :], r3[:, b, :].rearrange("p (c t) -> p c t", t=CH),
                        w3(12)[:, b, :].rearrange("p (c t) -> p c t", t=CH), MUL))
            link(V.tensor_copy(gend[:, :], by_chunk(w(12))[:, :, CH - 1]))
            link(tt(w(2), w(6), w(13), MUL))
            link(tt(w(3), w(5), w(13), MUL), scaled)
            dve.wait_ge(head_mm, 2)
            link(tt(w3(16), ps[6].rearrange("p (b t) -> p b t", b=NB), v3, MUL), rk_ready)
            def merge_square(k):
                link(tt(w3(17), mix3(k), mix3(k), MUL), mg_sq)

            def merge_scale(n, k):
                dve.wait_ge(mg_rstd, n + 1)
                for b in range(NB):
                    link(stt(mix_ap(k, b), mix_ap(k, b), pc("gain", 2 * k + b), rstd[:, :], MUL, MUL), mixed if b else v_own)

            dve.wait_ge(proj_kept, 6)
            dve.wait_ge(s5_tab, 1)
            for b in range(NB):
                link(ts(lru_x3[:, b, :], lxp[:, b, 0:SEQ], pc("conv", b), pc("conv_b", b), MUL, ADD))
            for j in range(1, 4):
                for b in range(NB):
                    link(stt(lru_x3[:, b, :], lxp[:, b, j:j + SEQ], pc("conv", 2 * j + b), lru_x3[:, b, :], MUL, ADD),
                         lr_xc if (j, b) == (3, 1) else v_own)
            dve.wait_ge(lr_sp, 1)
            link(ts(col[:, 2:4], col[:, 0:2], 8.0, None, MUL))
            link(ts(col[:, 4:6], col[:, 0:2], -8.0, None, MUL), lr_coef)
            dve.wait_ge(s5_trig, 1)
            sn, cs = ang[:, 0, :, :], ang[:, 1, :, :]

            for k in range(2):
                dve.wait_ge(score_mm, k + 1)
                for q in range(2):
                    src = ps[3 + 2 * k + q].rearrange("p (m r t) -> p m r t", m=4, r=2)
                    ms = slice(4 * q, 4 * q + 4)
                    link(tt(by_chunk(w(7 + k))[:, ms, :], src[:, :, 0, :], m_strict[:, :].unsqueeze(1).broadcast_to([P, 4, CH]), MUL))
                    link(tt(by_chunk(w(9 + k))[:, ms, :], src[:, :, 1, :], m_incl[:, :].unsqueeze(1).broadcast_to([P, 4, CH]), MUL), score_kept)
            def s5_states(q):
                j0 = 2 * q
                C2, S2 = cosT[:, j0:j0 + 2, :], sinT[:, j0:j0 + 2, :]
                dve.wait_ge(s5_bu, q + 2)
                if q:
                    dve.wait_ge(s5_x, q)
                for jj in range(2):
                    bank = ps[(2, 7)[jj]]
                    for out_k, in_k, tab in ((0, 0, C2), (2, 1, S2), (1, 1, C2), (3, 0, S2)):
                        ins = tt(s5t[out_k][:, jj, :], bank[:, in_k * SEQ:(in_k + 1) * SEQ], tab[:, jj, :], MUL)
                        link(ins, s5_rot if (jj, out_k) == (1, 3) else v_own)
                link(tt(s5t[0], s5t[0], s5t[2], ADD))
                link(tt(s5t[1], s5t[1], s5t[3], SUB))
                for jj in range(2):
                    mag = s5c[:, 1, j0 + jj:j0 + jj + 1].broadcast_to([P, SEQ])
                    link(V.tensor_tensor_scan(s5t[2][:, jj, :], mag, s5t[0][:, jj, :], 0.0, MUL, ADD))
                    link(V.tensor_tensor_scan(s5t[3][:, jj, :], mag, s5t[1][:, jj, :], 0.0, MUL, ADD), s5_scan if jj else v_own)
                if q:
                    dve.wait_ge(s5_y, q)
                link(tt(s5x[0], s5t[2], C2, MUL))
                link(tt(s5t[0], s5t[3], S2, MUL))
                link(tt(s5x[0], s5x[0], s5t[0], SUB), s5_xr)

            eye = ident64[:, :].unsqueeze(1).broadcast_to([P, NM, CH])

            def joined(l):
                link(tt(by_chunk(w(14)), by_chunk(w(7)), lev[:, l, :].unsqueeze(1).broadcast_to([P, NM, CH]), MUL), lev_m)

            joined(0)
            dve.wait_ge(lr_gates, 6)
            link(ts(lru_s, lru_s, 1e-18, None, ALU.max))
            link(ts(w(17), lru_s, 1.0, None, ADD))
            link(V.reciprocal(w(17), w(17)))
            link(stt(lru_s, lru_s, 2.0, w(17), MUL, MUL), lr_ln)
            link(tt(lru_i, lru_i, lru_x, MUL))
            dve.wait_ge(lev_p, 1)
            link(tt(by_chunk(w(11)), by_chunk(ps[3]), eye, ADD), lev_xk)
            link(tt(by_chunk(w(12)), by_chunk(w(14)), eye, ADD), lev_xk)
            for l in range(1, LEVELS):
                joined(l)
                if l == 1:
                    dve.wait_ge(lr_gates, 8)
                    link(V.memset(lru_a3[:, 1, 0:1], 0.0))
                    dve.wait_ge(lr_sq, 1)
                    link(tt(w(17), lru_i, lru_s, MUL))
                    link(V.tensor_tensor_scan(lru_x, lru_a, w(17), 0.0, MUL, ADD))
                    dve.wait_ge(lr_gelu, 1)
                    link(tt(flat(kept["lg"]), flat(kept["lg"]), lru_x, MUL))
                    merge_square(3)
                if l == 3:
                    merge_scale(0, 3)
                if l >= 2:
                    s5_states(l - 2)
                if l < LEVELS - 1:
                    dve.wait_ge(lev_x, 2 * l - 1)
                    link(tt(w(11), ps[4], w(11), ADD), lev_xk)
                    dve.wait_ge(lev_x, 2 * l)
                else:
                    dve.wait_ge(lev_x, 2 * l - 1)
                link(tt(w(12), ps[5], w(12), ADD), lev_xk)
            gend3 = gend[:, :].rearrange("p (b c) -> p b c", b=NB)
            for c in range(NCH):
                if 1 <= c < NCH - 1:
                    for b in range(NB):
                        link(ts(state_g[:, b, :], state[:, c % 2, b, :], gend3[:, b, c:c + 1], None, MUL))
                dve.wait_ge(ch_rhs, c + 1)
                link(V.tensor_copy(rhs_t[:, :, :].rearrange("p b t -> p (b t)"), ps[3][:, 0:P]), ch_rhsk)
                dve.wait_ge(ch_u, c + 1)
                link(V.tensor_copy(u_t[:, :, :].rearrange("p b t -> p (b t)"), ps[4][:, 0:P]), ch_uk)
                if c < NCH - 1:
                    dve.wait_ge(ch_s, c + 1)
                    for b in range(NB):
                        nxt, src, g = state[:, (c + 1) % 2, b, :], ps[5][:, b * CH:(b + 1) * CH], gend3[:, b, c:c + 1]
                        link(ts(nxt, src, g, None, MUL) if c == 0 else stt(nxt, src, g, state_g[:, b, :], MUL, ADD), ch_sk)
                if c == 1:
                    dve.wait_ge(s5_y, 4)
                    for b in range(NB):
                        link(stt(s5_act[:, b, :], kept["su"][:, b, :], pc("s5d", b), ps[6][:, b * SEQ:(b + 1) * SEQ], MUL, ADD),
                             s5_pre if b else v_own)
                if c == 2:
                    dve.wait_ge(hg_gates, 4)
                    link(ts(w(2), w(2), 1e-18, None, ALU.max), hg_f)

            hq, hf, hi, hg = (flat(kept[n]) for n in ("hq", "hf", "hi", "hg"))
            lam = w(11)

            def level_diff(k):
                L = HG_LEVELS[k]
                n = 512 // (2 * L)
                dk = w((8, 12)[k % 2])
                d, lp = (t.rearrange("p (n two l) -> p n two l", two=2, l=L) for t in (dk, lam))
                mid = lp[:, :, 0, L - 1:L]
                if L == 128:
                    link(tt(d[:, :, 0, :], lp[:, :, 0, :], mid.broadcast_to([P, n, L]), SUB))
                    link(V.tensor_copy(d[:, :, 1, :], lp[:, :, 1, :]), hg_diff)
                else:
                    link(tt(dk.rearrange("p (n l) -> p n l", l=2 * L), lam.rearrange("p (n l) -> p n l", l=2 * L),
                            mid.broadcast_to([P, n, 2 * L]), SUB), hg_diff)

            def level_scaled(k):
                L = HG_LEVELS[k]
                d, t, kk, qq = (t.rearrange("p (n two l) -> p n two l", two=2, l=L) for t in (w((8, 12)[k % 2]), w(k), hf, hq))
                dve.wait_ge(hg_e, 2 * k + 2)
                link(tt(t[:, :, 0, :], kk[:, :, 0, :], d[:, :, 0, :], MUL))
                link(tt(t[:, :, 1, :], qq[:, :, 1, :], d[:, :, 1, :], MUL), hg_scaled)

            acc, one = (w(k).rearrange("p (e n t) -> p e n t", e=2, n=4) for k in (14, 9))

            def level_masked(li):
                dve.wait_ge(hg_sc, li + 1)
                lb = LEVEL_BANK[li % 2]
                src = banks8[:, lb:lb + 2, 0:256].rearrange("p e (n t) -> p e n t", n=4)
                mask = lev[:, LEVELS + 1 - li, :].unsqueeze(1).unsqueeze(1).broadcast_to([P, 2, 4, CH])
                link(tt(one if li > 2 else acc, src, mask, MUL), hg_sck)
                if li > 2:
                    link(tt(w(14), w(14), w(9), ADD))

            dve.wait_ge(hg_ln, 1)
            cumulate(lam, w(2), P)
            level_diff(0)
            level_diff(1)
            dve.wait_ge(hg_gates, 5)
            dve.wait_ge(ch_y, NCH)
            level_scaled(0)
            level_diff(2)
            dve.wait_ge(gn_mm, 1)
            link(stt(w(17), ps[6], -1.0 / HEAD, w(17), MUL, ADD))
            link(tt(w(13), w(17), w(17), MUL), gn_sq)
            level_scaled(1)
            level_diff(3)
            dve.wait_ge(gn_rstd, 1)
            link(tt(w(17), w(17), w(14), MUL))
            for b in range(NB):
                link(ts(w3(17)[:, b, :], w3(17)[:, b, :], pc("ln_w", b), pc("ln_b", b), MUL, ADD))
            link(tt(w(17), w(17), w(16), ADD))
            link(tt(mix3(2), w3(17), w3(15), MUL))
            merge_square(2)
            link(V.memset(w(15, 2), 0.0))
            level_scaled(2)
            level_diff(4)
            level_scaled(3)
            level_diff(5)
            dve.wait_ge(s5_sig, 1)
            link(tt(kept["su"][:, :, :], ps[1].rearrange("p (b t) -> p b t", b=NB), s5_gate, MUL))
            level_masked(2)
            merge_scale(1, 2)
            merge_square(1)
            level_scaled(4)
            level_diff(6)
            level_masked(3)
            level_scaled(5)
            level_diff(7)
            level_masked(4)
            level_scaled(6)
            level_masked(5)
            merge_scale(2, 1)
            level_scaled(7)
            level_masked(6)
            link(tt(hf, hf, hq, MUL), hg_qk)
            level_masked(7)
            SC = w(15, 2).rearrange("p (e n t) -> p e n t", e=2, n=4)
            link(V.tensor_copy(SC[0:64, :, :, 0:64], acc[0:64]))
            link(V.tensor_copy(SC[64:128, :, :, 64:128], acc[64:128]))
            link(V.tensor_copy(SC[0:64, :, :, 64:128], banks8[0:64, 4:6, 256:512].rearrange("p e (n t) -> p e n t", n=4)))
            link(V.tensor_copy(w(13).rearrange("p (e t) -> p e t", e=2), banks8[:, 4:6, 0:SEQ]), hg_sck)
            dve.wait_ge(hg_qkmm, 1)
            link(tt(w(2), ps[3], hi, MUL))
            dve.wait_ge(hg_o, 1)
            link(tt(w(1), ps[6], w(2), ADD))
            link(tt(w(0), w(1), w(1), MUL), hg_osq)
            dve.wait_ge(hg_orstd, 1)
            link(tt(w(1), w(1), w(0), MUL))
            for b in range(NB):
                link(stt(kept["hg"][:, b, :], w3(1)[:, b, :], pc("hnorm", b), kept["hg"][:, b, :], MUL, MUL))
            merge_square(0)
            merge_scale(3, 0)

            dve.wait_ge(s_xnat, 32)
            for tb in range(TB):
                for n in range(2):
                    dve.wait_ge(wo_mm, 2 * tb + n + 1)
                    part = hN[:, tb, n * 512:(n + 1) * 512]
                    link(tt(part, ps[OUT_BANK[tb][n]], part, ADD), h_ready)
            dve.wait_ge(s_rows, 48)
            dve.wait_ge(consts, 6)
            for tb in range(TB):
                dve.wait_ge(n2_rstd, tb + 1)
                link(stt(x2[:, tb, :], hN[:, tb, :], col[:, 10 + tb:11 + tb], n2w, MUL, MUL), x2_ready)

            link(V.memset(Yb[:, 0:512], 0.0), y_k)
            link(V.memset(Yb[:, 512:1024], 0.0), y_k)
            link(V.memset(PWT, 0.0), pwt_k)
            link(V.memset(hT, 0.0), ht_k)

            cz = rt[:, 0:16].rearrange("p (b n) -> p b n", b=TB)
            mx = rt[:, 16:32].rearrange("p (b n) -> p b n", b=TB)
            ix = rt[:, 32:48].rearrange("p (b n) -> p b n", b=TB)
            ixu = ix.bitcast(U32)
            fs = rt[:, 48:64].rearrange("p (b n) -> p b n", b=TB)
            fmx = rt[:, 64:80].rearrange("p (b n) -> p b n", b=TB)
            fix = rt[:, 80:96].rearrange("p (b n) -> p b n", b=TB)
            fixu = fix.bitcast(U32)
            gs = rt[:, 96:98]
            oh = rt[:, 100:108].rearrange("p (b n) -> p b n", b=TB)
            fi = rt[:, 108:112].rearrange("p (b n) -> p b n", b=TB)
            sm = rt[:, 114:116]
            w0_, w1_ = rt[:, 116:118], rt[:, 118:120]
            df = work[:, 12, 96:112].rearrange("p (b n) -> p b n", b=TB)
            ex = work[:, 12, 80:96].rearrange("p (b n) -> p b n", b=TB)
            fine = lg[:, :, 4:36].rearrange("p b (g n) -> p b g n", g=N_COARSE)
            fprod = work[:, 15, 0:64].rearrange("p (b g n) -> p b g n", b=TB, g=N_COARSE)
            link(V.memset(rt[:, 0:16], -3e38))
            link(V.memset(work[:, 12, 96:112], 0.0))
            link(V.memset(C[:, :, 32:34], 0.0))
            link(V.memset(KEY[:, :, 32:34], -1.0))
            dve.wait_ge(logit_mm, 2)
            link(tt(lg, banks8[:, 6:8, 0:36], rout[:, DC * 36:].unsqueeze(1).broadcast_to([P, TB, 36]), ADD))
            link(V.tensor_copy(cz[:, :, 0:4], lg[:, :, 0:4]))
            for tb in range(TB):
                link(V.max(mx[:, tb, :], cz[:, tb, :]))
                link(V.max_index(ixu[:, tb, :], mx[:, tb, :], cz[:, tb, :]))
            link(V.tensor_copy(gs.unsqueeze(2), ixu[:, :, 0:1]))
            link(tt(oh, iota32[:, 0:4].unsqueeze(1).broadcast_to([P, TB, 4]), gs.unsqueeze(2).broadcast_to([P, TB, 4]), ALU.is_equal))
            for tb in range(TB):
                link(tt(fprod[:, tb], fine[:, tb], oh[:, tb, :].unsqueeze(2).broadcast_to([P, N_COARSE, PER_GROUP]), MUL))
            link(tt(fprod[:, :, 0:2, :], fprod[:, :, 0:2, :], fprod[:, :, 2:4, :], ADD))
            link(tt(fs, fprod[:, :, 0, :], fprod[:, :, 1, :], ADD))
            for tb in range(TB):
                link(V.max(fmx[:, tb, :], fs[:, tb, :]))
                link(V.max_index(fixu[:, tb, :], fmx[:, tb, :], fs[:, tb, :]))
            link(tt(df[:, :, 4:5], fmx[:, :, 1:2], fmx[:, :, 0:1], SUB))
            link(tt(df[:, :, 0:4], cz[:, :, 0:4], mx[:, :, 0:1].broadcast_to([P, TB, 4]), SUB), r_exp)
            link(V.tensor_copy(fi[:, :, :], fixu[:, :, 0:2]))
            link(stt(fi, gs.unsqueeze(2).broadcast_to([P, TB, 2]), float(PER_GROUP), fi, MUL, ADD))
            iota_b = iota32.unsqueeze(1).broadcast_to([P, TB, N_EXPERTS])
            link(tt(M0, iota_b, fi[:, :, 0:1].broadcast_to([P, TB, N_EXPERTS]), ALU.is_equal))
            link(tt(M1, iota_b, fi[:, :, 1:2].broadcast_to([P, TB, N_EXPERTS]), ALU.is_equal))
            link(tt(M, M0, M1, ADD), r_exp)
            dve.wait_ge(r_expd, 1)
            link(V.tensor_reduce(sm.unsqueeze(2), ex[:, :, 0:4], AX.X, ADD))
            link(stt(sm.unsqueeze(2), ex[:, :, 4:5], 1.0, sm.unsqueeze(2), ADD, MUL))
            link(V.reciprocal(w0_, sm))
            link(tt(w1_.unsqueeze(2), w0_.unsqueeze(2), ex[:, :, 4:5], MUL))
            for tb in range(TB):
                link(ts(C[:, tb, 0:32], M0[:, tb, :], w0_[:, tb:tb + 1], None, MUL))
                link(stt(C[:, tb, 0:32], M1[:, tb, :], w1_[:, tb:tb + 1], C[:, tb, 0:32], MUL, ADD))
            dve.wait_ge(rank_mm, 1)
            rank = ps[4][:, 0:64].rearrange("p (b e) -> p b e", b=TB)
            link(stt(KEY[:, :, 0:32], rank, 1.0, M, ADD, MUL))
            link(ts(KEY[:, :, 0:32], KEY[:, :, 0:32], -1.0, None, ADD), routed)
            iota4 = iota.unsqueeze(1).unsqueeze(1).broadcast_to([P, TB, 2, SLOTS])

            def one_hot(dst, i):
                return tt(dst.rearrange("p b (a s) -> p b a s", a=2), iota4,
                          KEY[:, :, bass.ds(i, 2)].unsqueeze(3).broadcast_to([P, TB, 2, SLOTS]), ALU.is_equal)

            link(one_hot(Pm, 0), p_ready)
            link(stt(CR, rank, float(SLOTS), C[:, :, 0:32], ALU.is_ge, MUL))
            link(V.tensor_reduce(col[0:1, 20:21], ps[4][0:1, 64:96], AX.X, ALU.max))
            link(ts(flag_i[0:1, 0:1], col[0:1, 20:21], float(SLOTS), None, ALU.is_gt), routed)

            with dve.Fori(0, PAIRS) as i:
                dve.wait_ge(gath_mm, i + 1)
                one_hot(Pm, i * 2 + 2).then_inc(p_ready, 1)
                dve.wait_ge(gate_done, i + 1)
                one_hot(PW, i * 2).then_inc(pw_half, 1)
                dve.wait_ge(pw_half, i + 1)
                tt(PW.rearrange("p b (a s) -> p b a s", a=2), PW.rearrange("p b (a s) -> p b a s", a=2),
                   C[:, :, bass.ds(i * 2, 2)].unsqueeze(3).broadcast_to([P, TB, 2, SLOTS]), MUL).then_inc(pw_ready, 1)
                dve.wait_ge(silu_k, i + 1)
                dve.wait_ge(up_done, i + 1)
                tt(hb, ps[5], sg, MUL).then_inc(h_k, 1)
                dve.wait_ge(ht_mm, i + 1)
                V.tensor_copy(hT.rearrange("p c s -> p (c s)"), ps[4]).then_inc(ht_k, 1)
                dve.wait_ge(pwt_mm, i + 1)
                V.tensor_copy(PWT, ps[5][:, 0:256]).then_inc(pwt_k, 1)
            for tb in range(TB):
                dve.wait_ge(y_mm, tb + 1)
                for n in range(2):
                    part = hN[:, tb, n * 512:(n + 1) * 512]
                    link(tt(part, ps[2 * tb + n], part, ADD), ysum if n else v_own)
            flag = dve.value_load(flag_i[0:1, 0:1], min_val=0, max_val=1)
            with dve.If(flag > 0):
                dve.wait_ge(dn_pe, 1)
                for tb in range(TB):
                    for q in range(2):
                        ins = V.tensor_copy(x2T[:, 4 * q:4 * q + 4, tb * P:(tb + 1) * P], ps[2 * tb + q].rearrange("p (c t) -> p c t", c=4))
                ins.then_inc(dn_dve, 1)
                with dve.Fori(0, N_EXPERTS) as e:
                    for tb in range(TB):
                        dve.wait_ge(dn_act, e * 2 + tb + 1)
                        tt(hb, ps[5], sg, MUL).then_inc(dn_own, 1)
                        dve.wait_ge(dn_own, e * 2 + tb + 1)
                        ts(hb, hb, CR[:, tb, bass.ds(e, 1)], None, MUL).then_inc(dn_dve, 1)
                        dve.wait_ge(dn_pe, e * 6 + 3 * tb + 3)
                        V.tensor_copy(hT.rearrange("p c s -> p (c s)"), ps[4]).then_inc(dn_dve, 1)
                        dve.wait_ge(dn_pe, e * 6 + 3 * tb + 4)
                        tt(hN[:, tb, 0:512], ps[6], hN[:, tb, 0:512], ADD)
                        tt(hN[:, tb, 512:1024], ps[7], hN[:, tb, 512:1024], ADD).then_inc(dn_dve, 1)
                dve.wait_ge(dn_dve, 6 * N_EXPERTS + 1)
                V.memset(col[:, 16:17], 0.0).then_inc(fin_sum, 1)
            with dve.Else():
                dve.nop()
            dve.wait_ge(fin_rstd, 1)
            for tb in range(TB):
                for n in range(2):
                    part, fw_n = hN[:, tb, n * 512:(n + 1) * 512], fw[:, n * 512:(n + 1) * 512]
                    link(stt(part, part, col[:, 14 + tb:15 + tb], fw_n, MUL, MUL), fin)


def kernel(**inputs):
    import numpy as np
    import concourse.bacc as bacc
    from concourse.bass_utils import run_bass_kernel_spmd

    a = {k: np.asarray(v) for k, v in inputs.items()}

    def columns(v, width=P):
        return v.reshape(-1, width).T

    state_cols = lambda v: v.reshape(S5_T, P).T
    params = {
        "norm1": columns(a["norm1_w"][0]), "w0": columns(a["rwkv_w0"][0]), "a0": columns(a["rwkv_a0"][0]),
        "k_k": columns(a["rwkv_k_k"][0]), "k_a": columns(a["rwkv_k_a"][0]), "r_k": columns(a["rwkv_r_k"][0]),
        "ln_w": columns(a["rwkv_ln_w"][0]), "ln_b": columns(a["rwkv_ln_b"][0]),
        "conv": columns(a["lru_conv_w"][0].reshape(-1)), "conv_b": columns(a["lru_conv_b"][0]),
        "ba": columns(a["lru_ba"][0]), "bx": columns(a["lru_bx"][0]), "lam": columns(a["lru_lambda"][0]),
        "hnorm": columns(a["hgrn_norm_w"][0]), "s5d": columns(a["s5_d"][0]), "gain": columns(a["merge_gain"][0]),
        "mu": columns(a["rwkv_mu"][0]), "lr": state_cols(a["s5_lambda_re"][0]), "li": state_cols(a["s5_lambda_im"][0]),
        "ldt": state_cols(np.repeat(a["s5_log_dt"][0], 64)),
    }
    router = np.concatenate([a["moe_coarse_w"][0], a["moe_fine_w"][0].transpose(1, 0, 2).reshape(D_MODEL, 32)], axis=1)
    rbias = np.concatenate([a["moe_coarse_b"][0], a["moe_fine_b"][0].reshape(-1)])

    def s5_b(v):
        return v.reshape(S5_T, P, S5_CH).transpose(1, 0, 2).reshape(P, -1)

    def heads(v):
        return v.reshape(NB, P, HEAD).transpose(1, 0, 2).reshape(P, -1)

    small = {
        "wa2": np.concatenate([a["rwkv_w2"][0], a["rwkv_a2"][0]]), "g2": a["rwkv_g2"][0],
        "lwa": heads(a["lru_wa"][0]), "lwx": heads(a["lru_wx"][0]),
        "bre": s5_b(a["s5_b_re"][0]), "bim": s5_b(a["s5_b_im"][0]),
        "cre": s5_b(a["s5_c_re"][0].transpose(0, 2, 1)), "cim": s5_b(a["s5_c_im"][0].transpose(0, 2, 1)),
    }
    w_in = a["w_in"][0]
    pieces = [w_in[:, FIRST_COLUMN[g]:FIRST_COLUMN[g] + 256].reshape(DC, P, 256).transpose(1, 0, 2) for g in GROUPS]
    arrays = {
        "x": a["x"][0],
        "xT": a["x"][0].T.reshape(DC, P, SEQ).transpose(1, 0, 2).reshape(P, -1),
        "params": np.concatenate([params[n] for n, _ in PARAMS], axis=1),
        "small": np.concatenate([small[n] for n, _ in SMALL], axis=1),
        "glu": a["s5_w_glu"][0].reshape(NB, P, 512).transpose(1, 0, 2).reshape(P, -1),
        "router": np.concatenate([router.reshape(DC, P, 36).transpose(1, 0, 2).reshape(P, -1), np.broadcast_to(rbias, (P, 36))], axis=1),
        "w_in": np.stack(pieces),
        "w_out": a["w_out"][0], "norm2_w": a["norm2_w"][0], "final_w": a["final_norm_w"],
        "w_gate": a["moe_w_gate"][0], "w_up": a["moe_w_up"][0], "w_down": a["moe_w_down"][0],
    }
    nc = bacc.Bacc("TRN2", target_bir_lowering=False, num_devices=1)
    feed, args = {}, []
    for name, v in arrays.items():
        v = np.ascontiguousarray(v)
        feed[f"in_{name}"] = v
        args.append(nc.dram_tensor(f"in_{name}", v.shape, mybir.dt.from_np(v.dtype), kind="ExternalInput").ap())
    out = nc.dram_tensor("out_0", (SEQ, D_MODEL), F32, kind="ExternalOutput").ap()
    build_layer(nc, *args, out)
    r = run_bass_kernel_spmd(nc, [feed], core_ids=[0])
    return np.asarray(r.results[0]["out_0"]).reshape(1, SEQ, D_MODEL)
```
